# Optimizing a Trainium2 kernel written in Bass

```python
import math
import jax, jax.numpy as jnp
from jax import lax
import numpy as np

D_MODEL = 1024
BATCH = 1
SEQ = 512
DEPTH = 2

N_A_LAYERS = DEPTH // 2
N_B_LAYERS = DEPTH - N_A_LAYERS
D_FF = 2816
RWKV_HEAD = 64
RWKV_HEADS = D_MODEL // RWKV_HEAD
LORA_DECAY = 64
LORA_AAA = 64
LORA_GATE = 160
RWKV_LN_EPS = 64e-5
N_SHIFT_MIX = 6
DIFF_HEAD = 64
DIFF_HEADS = D_MODEL // (2 * DIFF_HEAD)
DIFF_V_HEAD = 2 * DIFF_HEAD
Q_BLOCK = 128
NORM_EPS = 1e-6
SUBLN_EPS = 1e-5


def rms_norm(x, g, eps=NORM_EPS):
    xf = x.astype(jnp.float32)
    y = xf * lax.rsqrt(jnp.mean(xf * xf, axis=-1, keepdims=True) + eps)
    return (y * g.astype(jnp.float32)).astype(x.dtype)

def swiglu(h, w_in, w_out):
    gate, up = jnp.split(h @ w_in, 2, axis=-1)
    return (jax.nn.silu(gate) * up) @ w_out

def lambda_init(layer_idx):
    return 0.8 - 0.6 * math.exp(-0.3 * layer_idx)

def alibi_slopes(n_heads):
    return 2.0 ** (-8.0 * jnp.arange(1, n_heads + 1, dtype=jnp.float32) / n_heads)

def wkv7_scan(r, decay, k, v, a, b):
    B, T, H, N = r.shape

    def step(S, inp):
        r_t, w_t, k_t, v_t, a_t, b_t = inp
        sa = jnp.einsum('bhij,bhj->bhi', S, a_t)
        S = S * w_t[:, :, None, :] + sa[..., None] * b_t[:, :, None, :] + v_t[..., None] * k_t[:, :, None, :]
        return S, jnp.einsum('bhij,bhj->bhi', S, r_t)

    xs = [jnp.moveaxis(t.astype(jnp.float32), 1, 0) for t in (r, decay, k, v, a, b)]
    S0 = jnp.zeros((B, H, N, N), jnp.float32)
    _, y = lax.scan(step, S0, xs)
    return jnp.moveaxis(y, 0, 1)

def rwkv7_time_mix(h, mu, w_rkv, w0, w1, w2, a0, a1, a2, g1, g2, k_k, k_a, r_k, ln_g, ln_b, w_o):
    B, T, C = h.shape
    H, N = RWKV_HEADS, RWKV_HEAD
    h_prev = jnp.pad(h, ((0, 0), (1, 0), (0, 0)))[:, :-1]
    dx = h_prev - h
    r, k, v = jnp.einsum('sbtc,scd->sbtd', h[None] + dx[None] * mu[:3, None, None, :], w_rkv)
    xw = h + dx * mu[3]
    xa = h + dx * mu[4]
    xg = h + dx * mu[5]
    w_log = -jax.nn.softplus(-(w0 + jnp.tanh(xw @ w1) @ w2)) - 0.5
    decay = jnp.exp(-jnp.exp(w_log.astype(jnp.float32)))
    a = jax.nn.sigmoid(a0 + (xa @ a1) @ a2)
    g = jax.nn.sigmoid(xg @ g1) @ g2
    kk = (k * k_k).reshape(B, T, H, N).astype(jnp.float32)
    kk = kk * lax.rsqrt(jnp.maximum(jnp.sum(kk * kk, axis=-1, keepdims=True), 1e-24))
    k = k * (1 + (a - 1) * k_a)
    heads = lambda t: t.reshape(B, T, H, N)
    a_h = heads(a).astype(jnp.float32)
    y = wkv7_scan(heads(r), heads(decay), heads(k), heads(v), -kk, kk * a_h)
    mean = jnp.mean(y, axis=-1, keepdims=True)
    var = jnp.mean(jnp.square(y - mean), axis=-1, keepdims=True)
    y = ((y - mean) * lax.rsqrt(var + RWKV_LN_EPS)).reshape(B, T, C) * ln_g + ln_b
    bonus = jnp.sum(heads(r).astype(jnp.float32) * heads(k).astype(jnp.float32) * r_k, axis=-1, keepdims=True)
    y = y + (bonus * heads(v).astype(jnp.float32)).reshape(B, T, C)
    return (y.astype(h.dtype) * g) @ w_o

def shared_kv(x, kv_norm, w_kv, k_norm):
    B, T, _ = x.shape
    kv = rms_norm(x, kv_norm) @ w_kv
    k = rms_norm(kv[..., :D_MODEL].reshape(B, T, DIFF_HEADS, 2, DIFF_HEAD), k_norm).transpose(0, 2, 3, 1, 4)
    v = kv[..., D_MODEL:].reshape(B, T, DIFF_HEADS, DIFF_V_HEAD).transpose(0, 2, 1, 3)
    return k, v

def diff_attention(h, k_sh, v_sh, w_q, q_norm, lam, subln, w_o, lam_init):
    B, T, _ = h.shape
    H, d = DIFF_HEADS, DIFF_HEAD
    n_blk = T // Q_BLOCK
    q = rms_norm((h @ w_q).reshape(B, T, H, 2, d), q_norm)
    q = q.reshape(B, n_blk, Q_BLOCK, H, 2, d).transpose(1, 0, 3, 4, 2, 5)
    lamf = lam.astype(jnp.float32)
    lam_full = jnp.exp(jnp.sum(lamf[0] * lamf[1])) - jnp.exp(jnp.sum(lamf[2] * lamf[3])) + lam_init
    slopes = alibi_slopes(H)
    k_pos = jnp.arange(T, dtype=jnp.int32)
    scale = d ** -0.5

    def block(args):
        qb, start = args
        s = jnp.einsum('bhcqd,bhckd->bhcqk', qb, k_sh).astype(jnp.float32) * scale
        dist = (start + jnp.arange(Q_BLOCK, dtype=jnp.int32))[:, None] - k_pos[None, :]
        bias = -slopes[:, None, None] * dist.astype(jnp.float32)
        s = jnp.where(dist >= 0, s + bias[None, :, None], -jnp.inf)
        p = jax.nn.softmax(s, axis=-1)
        attn = p[:, :, 0] - lam_full * p[:, :, 1]
        return jnp.einsum('bhqk,bhkd->bhqd', attn.astype(v_sh.dtype), v_sh)

    starts = jnp.arange(n_blk, dtype=jnp.int32) * Q_BLOCK
    o = lax.map(block, (q, starts))
    o = rms_norm(o, subln, SUBLN_EPS) * (1.0 - lam_init)
    o = o.transpose(1, 0, 3, 2, 4).reshape(B, T, H * DIFF_V_HEAD)
    return o @ w_o

def first_inputs(seed: int = 0) -> dict:
    key = jax.random.key(seed)
    ks = jax.random.split(key, 29)
    C, F = D_MODEL, D_FF
    nA, nB = N_A_LAYERS, N_B_LAYERS
    nrm = lambda k, shape, s: jax.random.normal(k, shape, jnp.float32) * s
    gain = lambda k, shape: 1.0 + nrm(k, shape, 0.02)
    return {
        "x": nrm(ks[0], (BATCH, SEQ, C), 1.0),
        "ffn_norm": gain(ks[1], (DEPTH, 2, C)),
        "ffn_w_in": nrm(ks[2], (DEPTH, 2, C, 2 * F), C ** -0.5),
        "ffn_w_out": nrm(ks[3], (DEPTH, 2, F, C), F ** -0.5),
        "mix_norm": gain(ks[4], (DEPTH, C)),
        "rwkv_mu": jax.random.uniform(ks[5], (nA, N_SHIFT_MIX, C), jnp.float32),
        "rwkv_w_rkv": nrm(ks[6], (nA, 3, C, C), C ** -0.5),
        "rwkv_w0": jax.random.uniform(ks[7], (nA, C), jnp.float32, -6.0, -1.0),
        "rwkv_w1": nrm(ks[8], (nA, C, LORA_DECAY), C ** -0.5),
        "rwkv_w2": nrm(ks[9], (nA, LORA_DECAY, C), 0.5 * LORA_DECAY ** -0.5),
        "rwkv_a0": nrm(ks[10], (nA, C), 0.1),
        "rwkv_a1": nrm(ks[11], (nA, C, LORA_AAA), C ** -0.5),
        "rwkv_a2": nrm(ks[12], (nA, LORA_AAA, C), 0.5 * LORA_AAA ** -0.5),
        "rwkv_g1": nrm(ks[13], (nA, C, LORA_GATE), C ** -0.5),
        "rwkv_g2": nrm(ks[14], (nA, LORA_GATE, C), LORA_GATE ** -0.5),
        "rwkv_k_k": 0.85 + nrm(ks[15], (nA, C), 0.02),
        "rwkv_k_a": gain(ks[16], (nA, C)),
        "rwkv_r_k": nrm(ks[17], (nA, RWKV_HEADS, RWKV_HEAD), 0.1),
        "rwkv_ln_g": gain(ks[18], (nA, C)),
        "rwkv_ln_b": nrm(ks[19], (nA, C), 0.02),
        "rwkv_w_o": nrm(ks[20], (nA, C, C), 0.5 * C ** -0.5),
        "kv_norm": gain(ks[21], (C,)),
        "w_kv": nrm(ks[22], (C, 2 * C), C ** -0.5),
        "k_norm": gain(ks[23], (DIFF_HEAD,)),
        "diff_w_q": nrm(ks[24], (nB, C, C), C ** -0.5),
        "diff_q_norm": gain(ks[25], (nB, DIFF_HEAD)),
        "diff_lambda": nrm(ks[26], (nB, 4, DIFF_HEAD), 0.1),
        "diff_subln": gain(ks[27], (nB, DIFF_V_HEAD)),
        "diff_w_o": nrm(ks[28], (nB, C, C), 0.5 * C ** -0.5),
    }

def first_block(x, ffn_norm, ffn_w_in, ffn_w_out, mix_norm, rwkv_mu, rwkv_w_rkv, rwkv_w0, rwkv_w1, rwkv_w2,
              rwkv_a0, rwkv_a1, rwkv_a2, rwkv_g1, rwkv_g2, rwkv_k_k, rwkv_k_a, rwkv_r_k, rwkv_ln_g, rwkv_ln_b,
              rwkv_w_o, kv_norm, w_kv, k_norm, diff_w_q, diff_q_norm, diff_lambda, diff_subln, diff_w_o):
    k_sh = None
    v_sh = None
    for l in range(DEPTH):
        x = x + 0.5 * swiglu(rms_norm(x, ffn_norm[l, 0]), ffn_w_in[l, 0], ffn_w_out[l, 0])
        h = rms_norm(x, mix_norm[l])
        if l < N_A_LAYERS:
            i = l
            x = x + rwkv7_time_mix(h, rwkv_mu[i], rwkv_w_rkv[i], rwkv_w0[i], rwkv_w1[i], rwkv_w2[i],
                                   rwkv_a0[i], rwkv_a1[i], rwkv_a2[i], rwkv_g1[i], rwkv_g2[i],
                                   rwkv_k_k[i], rwkv_k_a[i], rwkv_r_k[i], rwkv_ln_g[i], rwkv_ln_b[i], rwkv_w_o[i])
        else:
            j = l - N_A_LAYERS
            x = x + diff_attention(h, k_sh, v_sh, diff_w_q[j], diff_q_norm[j], diff_lambda[j],
                                   diff_subln[j], diff_w_o[j], lambda_init(l))
        x = x + 0.5 * swiglu(rms_norm(x, ffn_norm[l, 1]), ffn_w_in[l, 1], ffn_w_out[l, 1])
        if l == N_A_LAYERS - 1:
            k_sh, v_sh = shared_kv(x, kv_norm, w_kv, k_norm)
    return x


DEPTH_2 = 1

GRID_W = 64
CTX_LEN = 256
MLA_HEADS = 8
MLA_NOPE = 64
MLA_ROPE = 32
MLA_V = 64
Q_LORA = 256
KV_LORA = 128
MLA_WIDTH = MLA_HEADS * MLA_V
NA_HEADS = 8
NA_DIM = 64
NA_KR = 8
NA_KC = 16
NA_WIDTH = NA_HEADS * NA_DIM

ROPE_THETA = 10000.0
EPS = 1e-6

KV_SPLITS = (KV_LORA, MLA_ROPE, NA_WIDTH, NA_WIDTH)
Q_SPLITS = (Q_LORA, MLA_WIDTH, NA_WIDTH, NA_WIDTH, D_MODEL, D_MODEL)
KV_COLS = KV_LORA + MLA_ROPE + 2 * NA_WIDTH
IN_WIDTH = KV_COLS + Q_LORA + MLA_WIDTH + 2 * NA_WIDTH + 2 * D_MODEL


def rmsnorm(x, g):
    xf = x.astype(jnp.float32)
    y = xf * lax.rsqrt(jnp.mean(xf * xf, axis=-1, keepdims=True) + EPS)
    return (y * g.astype(jnp.float32)).astype(x.dtype)

def split_cols(p, sizes):
    idx = np.cumsum(np.array(sizes))[:-1].tolist()
    return jnp.split(p, idx, axis=-1)

def heads(t, n):
    b, s, _ = t.shape
    return t.reshape(b, s, n, -1)

def rope_1d(x, pos):
    half = x.shape[-1] // 2
    freqs = ROPE_THETA ** (-jnp.arange(half, dtype=jnp.float32) / half)
    ang = pos.astype(jnp.float32)[:, None] * freqs[None, :]
    cos = jnp.cos(ang)[None, :, None, :]
    sin = jnp.sin(ang)[None, :, None, :]
    x1 = x[..., :half].astype(jnp.float32)
    x2 = x[..., half:].astype(jnp.float32)
    out = jnp.concatenate([x1 * cos - x2 * sin, x2 * cos + x1 * sin], axis=-1)
    return out.astype(x.dtype)

def rope_2d(x, rows, cols):
    d = x.shape[-1] // 2
    return jnp.concatenate([rope_1d(x[..., :d], rows), rope_1d(x[..., d:], cols)], axis=-1)

def mla_q(cq, g_cq, w_uq):
    b, s, _ = cq.shape
    q = (rmsnorm(cq, g_cq) @ w_uq).reshape(b, s, MLA_HEADS, MLA_NOPE + MLA_ROPE)
    return q[..., :MLA_NOPE], q[..., MLA_NOPE:]

def mla_kv(ckv, g_ckv, w_ukv):
    b, s, _ = ckv.shape
    kv = (rmsnorm(ckv, g_ckv) @ w_ukv).reshape(b, s, MLA_HEADS, MLA_NOPE + MLA_V)
    return kv[..., :MLA_NOPE], kv[..., MLA_NOPE:]

def block_attention(q, k, v, scale):
    b, s, h, dk = q.shape
    dv = v.shape[-1]
    nb = s // Q_BLOCK
    qb = q.reshape(b, nb, Q_BLOCK, h, dk).transpose(1, 0, 2, 3, 4)

    def one(qblk):
        sc = jnp.einsum('bqhd,bkhd->bhqk', qblk, k, preferred_element_type=jnp.float32) * scale
        p = jax.nn.softmax(sc, axis=-1).astype(v.dtype)
        return jnp.einsum('bhqk,bkhd->bqhd', p, v)

    o = lax.map(one, qb)
    return o.transpose(1, 0, 2, 3, 4).reshape(b, s, h * dv)

def neighborhood_attention(q, k, v, kc, vc, rpb):
    b, s, h, d = q.shape
    rows = s // GRID_W
    kr = min(NA_KR, rows)
    qg = q.reshape(b, rows, GRID_W, h, d)
    kg = k.reshape(b, rows, GRID_W, h, d)
    vg = v.reshape(b, rows, GRID_W, h, d)
    col = jnp.arange(GRID_W)
    c_start = jnp.clip(col - NA_KC // 2, 0, GRID_W - NA_KC)
    c_idx = c_start[:, None] + jnp.arange(NA_KC)[None, :]
    c_off = c_idx - col[:, None] + (NA_KC - 1)
    scale = d ** -0.5

    def one_row(r):
        r_start = jnp.clip(r - kr // 2, 0, rows - kr)
        k_slab = lax.dynamic_slice_in_dim(kg, r_start, kr, axis=1)
        v_slab = lax.dynamic_slice_in_dim(vg, r_start, kr, axis=1)
        k_win = k_slab[:, :, c_idx]
        v_win = v_slab[:, :, c_idx]
        qr = lax.dynamic_index_in_dim(qg, r, axis=1, keepdims=False)
        r_off = r_start + jnp.arange(kr) - r + (NA_KR - 1)
        bias = rpb[:, r_off[:, None, None], c_off[None, :, :]]
        bias = bias.transpose(0, 2, 1, 3).reshape(h, GRID_W, kr * NA_KC).astype(jnp.float32)
        s_win = jnp.einsum('bwhd,brwchd->bhwrc', qr, k_win, preferred_element_type=jnp.float32)
        s_win = s_win.reshape(b, h, GRID_W, kr * NA_KC) * scale + bias[None]
        s_ctx = jnp.einsum('bwhd,blhd->bhwl', qr, kc, preferred_element_type=jnp.float32) * scale
        p = jax.nn.softmax(jnp.concatenate([s_win, s_ctx], axis=-1), axis=-1).astype(v.dtype)
        p_win = p[..., :kr * NA_KC].reshape(b, h, GRID_W, kr, NA_KC)
        p_ctx = p[..., kr * NA_KC:]
        return (jnp.einsum('bhwrc,brwchd->bwhd', p_win, v_win)
                + jnp.einsum('bhwl,blhd->bwhd', p_ctx, vc))

    o = lax.map(one_row, jnp.arange(rows))
    return o.transpose(1, 0, 2, 3, 4).reshape(b, s, h * d)

def second_inputs(seed: int = 0) -> dict:
    key = jax.random.key(seed)
    ks = jax.random.split(key, 20)
    n = jax.random.normal
    D = D_MODEL
    return {
        "x": n(ks[0], (BATCH, SEQ, D), jnp.float32),
        "c": n(ks[1], (BATCH, D), jnp.float32),
        "ctx": n(ks[2], (BATCH, CTX_LEN, D), jnp.float32),
        "c_ctx": n(ks[3], (D,), jnp.float32),
        "w_mod": n(ks[4], (DEPTH_2, D, 3 * D), jnp.float32) * (0.5 * D ** -0.5),
        "b_mod": n(ks[5], (DEPTH_2, 3 * D), jnp.float32) * 0.01,
        "norm_g": 1.0 + 0.05 * n(ks[6], (DEPTH_2, D), jnp.float32),
        "w_in": n(ks[7], (DEPTH_2, D, IN_WIDTH), jnp.float32) * D ** -0.5,
        "g_cq": 1.0 + 0.05 * n(ks[8], (DEPTH_2, Q_LORA), jnp.float32),
        "w_uq": n(ks[9], (DEPTH_2, Q_LORA, MLA_HEADS * (MLA_NOPE + MLA_ROPE)), jnp.float32) * Q_LORA ** -0.5,
        "g_ckv": 1.0 + 0.05 * n(ks[10], (DEPTH_2, KV_LORA), jnp.float32),
        "w_ukv": n(ks[11], (DEPTH_2, KV_LORA, MLA_HEADS * (MLA_NOPE + MLA_V)), jnp.float32) * KV_LORA ** -0.5,
        "rpb": 0.02 * n(ks[12], (DEPTH_2, NA_HEADS, 2 * NA_KR - 1, 2 * NA_KC - 1), jnp.float32),
        "w_oa": n(ks[13], (DEPTH_2, MLA_WIDTH, D), jnp.float32) * MLA_WIDTH ** -0.5,
        "w_ob": n(ks[14], (DEPTH_2, NA_WIDTH, D), jnp.float32) * NA_WIDTH ** -0.5,
        "w_out": n(ks[15], (DEPTH_2, D, D), jnp.float32) * D ** -0.5,
        "final_g": 1.0 + 0.05 * n(ks[16], (D,), jnp.float32),
    }

def second_block(x, c, ctx, c_ctx, w_mod, b_mod, norm_g, w_in, g_cq, w_uq, g_ckv, w_ukv,
              rpb, w_oa, w_ob, w_out, final_g):
    b, s, _ = x.shape
    t = jnp.arange(s)
    row_pos = t // GRID_W
    col_pos = t % GRID_W
    mla_scale = (MLA_NOPE + MLA_ROPE) ** -0.5
    na_scale = NA_DIM ** -0.5
    sc = jax.nn.silu(c)
    scc = jax.nn.silu(c_ctx)
    for i in range(DEPTH_2):
        last = i == DEPTH_2 - 1
        shift, scale, gate = jnp.split((sc @ w_mod[i] + b_mod[i])[:, None, :], 3, axis=-1)
        shift_c, scale_c, gate_c = jnp.split(scc @ w_mod[i] + b_mod[i], 3, axis=-1)
        h = rmsnorm(x, norm_g[i]) * (1 + scale) + shift
        hc = rmsnorm(ctx, norm_g[i]) * (1 + scale_c) + shift_c

        ckv, kr, kb, vb, cq, za, qb, zb, ga, gb = split_cols(h @ w_in[i], KV_SPLITS + Q_SPLITS)
        if last:
            c_ckv, c_kr, c_kb, c_vb = split_cols(hc @ w_in[i][:, :KV_COLS], KV_SPLITS)
        else:
            (c_ckv, c_kr, c_kb, c_vb, c_cq, c_za, c_qb, c_zb, c_ga, c_gb) = split_cols(
                hc @ w_in[i], KV_SPLITS + Q_SPLITS)

        qa_n, qa_r = mla_q(cq, g_cq[i], w_uq[i])
        qa = jnp.concatenate([qa_n, rope_2d(qa_r, row_pos, col_pos)], axis=-1)
        ka_n, va = mla_kv(ckv, g_ckv[i], w_ukv[i])
        ka_r = rope_2d(kr[:, :, None, :], row_pos, col_pos)
        ka = jnp.concatenate([ka_n, jnp.broadcast_to(ka_r, ka_n.shape[:-1] + (MLA_ROPE,))], axis=-1)
        kca_n, vca = mla_kv(c_ckv, g_ckv[i], w_ukv[i])
        kca = jnp.concatenate(
            [kca_n, jnp.broadcast_to(c_kr[:, :, None, :], kca_n.shape[:-1] + (MLA_ROPE,))], axis=-1)
        oa = block_attention(qa, jnp.concatenate([ka, kca], axis=1),
                             jnp.concatenate([va, vca], axis=1), mla_scale)

        ob = neighborhood_attention(heads(qb, NA_HEADS), heads(kb, NA_HEADS), heads(vb, NA_HEADS),
                                    heads(c_kb, NA_HEADS), heads(c_vb, NA_HEADS), rpb[i])

        ya = (oa * jax.nn.silu(za)) @ w_oa[i]
        yb = (ob * jax.nn.silu(zb)) @ w_ob[i]
        y = (jax.nn.sigmoid(ga) * ya + jax.nn.sigmoid(gb) * yb) @ w_out[i]

        if not last:
            qca_n, qca_r = mla_q(c_cq, g_cq[i], w_uq[i])
            oca = block_attention(jnp.concatenate([qca_n, qca_r], axis=-1), kca, vca, mla_scale)
            ocb = block_attention(heads(c_qb, NA_HEADS), heads(c_kb, NA_HEADS),
                                  heads(c_vb, NA_HEADS), na_scale)
            yca = (oca * jax.nn.silu(c_za)) @ w_oa[i]
            ycb = (ocb * jax.nn.silu(c_zb)) @ w_ob[i]
            yc = (jax.nn.sigmoid(c_ga) * yca + jax.nn.sigmoid(c_gb) * ycb) @ w_out[i]
            ctx = ctx + gate_c * yc

        x = x + gate * y
    return rmsnorm(x, final_g)


def setup_inputs(seed=0):
    out = dict(first_inputs(seed))
    for name, value in second_inputs(seed + 1).items():
        if name != "x":
            out[name + "_2"] = value
    return out


def reference(
    x, ffn_norm, ffn_w_in, ffn_w_out, mix_norm, rwkv_mu, rwkv_w_rkv, rwkv_w0, rwkv_w1, rwkv_w2,
    rwkv_a0, rwkv_a1, rwkv_a2, rwkv_g1, rwkv_g2, rwkv_k_k, rwkv_k_a, rwkv_r_k, rwkv_ln_g,
    rwkv_ln_b, rwkv_w_o, kv_norm, w_kv, k_norm, diff_w_q, diff_q_norm, diff_lambda, diff_subln,
    diff_w_o, c_2, ctx_2, c_ctx_2, w_mod_2, b_mod_2, norm_g_2, w_in_2, g_cq_2, w_uq_2, g_ckv_2,
    w_ukv_2, rpb_2, w_oa_2, w_ob_2, w_out_2, final_g_2,
):
    x = first_block(
        x, ffn_norm, ffn_w_in, ffn_w_out, mix_norm, rwkv_mu, rwkv_w_rkv, rwkv_w0, rwkv_w1,
        rwkv_w2, rwkv_a0, rwkv_a1, rwkv_a2, rwkv_g1, rwkv_g2, rwkv_k_k, rwkv_k_a, rwkv_r_k,
        rwkv_ln_g, rwkv_ln_b, rwkv_w_o, kv_norm, w_kv, k_norm, diff_w_q, diff_q_norm,
        diff_lambda, diff_subln, diff_w_o,
    )
    return second_block(
        x, c_2, ctx_2, c_ctx_2, w_mod_2, b_mod_2, norm_g_2, w_in_2, g_cq_2, w_uq_2, g_ckv_2,
        w_ukv_2, rpb_2, w_oa_2, w_ob_2, w_out_2, final_g_2,
    )


_drawn_inputs = setup_inputs


def setup_inputs(seed=0):
    import zlib

    import numpy as np

    out = dict(_drawn_inputs(seed))
    spreads = {}
    factors = {'ffn_norm': 3.217,
     'mix_norm': 4.511,
     'rwkv_w1': 8.0,
     'rwkv_w2': 8.0,
     'rwkv_a0': 4.823,
     'rwkv_k_k': 64.0,
     'rwkv_k_a': 8.0,
     'rwkv_ln_g': 53.89,
     'rwkv_ln_b': 50.595,
     'kv_norm': 6.767,
     'k_norm': 8.0,
     'diff_q_norm': 8.0,
     'diff_subln': 64.0,
     'ctx_2': 7.004,
     'c_ctx_2': 2.956,
     'b_mod_2': 8.0,
     'norm_g_2': 8.0,
     'g_cq_2': 8.0,
     'w_uq_2': 6.849,
     'g_ckv_2': 8.0,
     'rpb_2': 64.0}
    for name, (base, spread) in spreads.items():
        noise = np.random.default_rng([zlib.crc32(name.encode()), seed]).standard_normal(out[name].shape)
        drawn = base * np.exp(spread * noise) if base else spread * noise
        out[name] = __import__('jax').numpy.asarray(drawn.astype(out[name].dtype))
    for name, factor in factors.items():
        out[name] = (out[name] * factor).astype(out[name].dtype)
    return out
```

```python
import math
from contextlib import ExitStack

import numpy as np

import concourse.bass as bass
from concourse import mybir

F32 = mybir.dt.float32
F32R = mybir.dt.float32r
ALU = mybir.AluOpType
ACT = mybir.ActivationFunctionType
AX_X = mybir.AxisListType.X

P = 128
C = 1024
KC = C // P
T = 512
TB = T // P
F = 2816
KF = F // P
CTX = 256
HEAD = 64
CHUNK = 64
NCH = T // CHUNK
DIFF_HEADS = 8
MLA_HEADS, NOPE, ROPE, MLA_V = 8, 64, 32, 64
QK = NOPE + ROPE
NA_HEADS, NA_KC, GRID_W, NA_KR = 8, 16, 64, 8
NA_OFF = 2 * NA_KR - 2
KEYS = T + CTX
NEG = -1.0e30

PACK1 = [("ffn_norm", 32), ("mix_norm", 16), ("rwkv_mu", 48)]
PACK2 = [("rwkv_w0", 8), ("rwkv_a0", 8), ("rwkv_k_k", 8), ("rwkv_k_a", 8), ("rwkv_r_k", 8),
         ("rwkv_ln_g", 8), ("rwkv_ln_b", 8), ("kv_norm", 8), ("norm_g_2", 8), ("final_g_2", 8),
         ("b_mod_2", 24), ("diff_subln", 1), ("g_cq_2", 2), ("g_ckv_2", 1), ("c_2", 8),
         ("c_ctx_2", 8), ("diff_q_norm", 1), ("k_norm", 1)]


class Queue:

    def __init__(self, sem):
        self.sem, self.count, self.items, self.waited = sem, 0, [], {}

    def wait(self, *marks):
        for m in marks:
            if m is None:
                continue
            if isinstance(m, list):
                self.wait(*m)
                continue
            sem, value = m
            if self.waited.get(id(sem), 0) < value:
                self.waited[id(sem)] = value
                self.items.append((None, (sem, value), {}, None))

    def op(self, issue, after, *args, **kw):
        self.wait(after)
        self.count += 1
        self.items.append((issue, args, kw, (self.sem, 1)))
        return (self.sem, self.count)

    def quiet(self, issue, after, *args, **kw):
        self.wait(after)
        self.items.append((issue, args, kw, None))

    def dma(self, issue, out, in_, counter, *after):
        self.wait(*after)
        counter[1] += 16
        self.items.append((issue, (out, in_), {}, (counter[0], 16)))
        return (counter[0], counter[1])

    def now(self):
        return (self.sem, self.count) if self.count else None

    def emit(self, engine):
        for issue, args, kw, inc in self.items:
            if issue is None:
                engine.wait_ge(*args)
                continue
            made = issue(*args, **kw)
            if inc:
                made.then_inc(*inc)


class Weights:

    RAW, CONV, AHEAD = 4, 4, 3

    def __init__(self, nc, raw, hi, lo, counters, sp, act, dve):
        self.nc, self.raw, self.hi, self.lo, self.counters = nc, raw, hi, lo, counters
        self.sp, self.act, self.dve = sp, act, dve
        self.units, self.prepared, self.nconv = [], 0, 0
        self.raw_free = [None] * self.RAW
        self.conv_free = [None] * self.CONV

    def plan(self, rows, blocks, direct=False, nk=2):
        out = []
        for cols in blocks:
            ids, k = [], 0
            while k * P < rows:
                n = min(nk, (rows - k * P) // P) or 1
                part = min(P, rows - k * P)
                self.units.append(dict(k0=k, nk=n, part=part, cols=cols, direct=direct))
                ids.append(len(self.units) - 1)
                k += n
            out.append(ids)
        return out

    def _prepare(self, i):
        u = self.units[i]
        slot, n, p, at = i % self.RAW, u["nk"], u["part"], 0
        for view in u["cols"]:
            src = view(u["k0"] * P, n * p, p)
            width = int(np.prod(src.shape[2:]))
            dst = self.raw[0:p, slot, 0:n, at:at + width]
            if n == 1:
                dst, src = dst[:, 0], src[:, 0]
            if len(src.shape) == 3 and n == 1:
                dst = dst.rearrange("p (a b) -> p a b", b=src.shape[2])
            arrived = self.sp.dma(self.nc.sync.dma_start, dst, src, self.counters[slot], self.raw_free[slot])
            at += width
        u["width"], u["raw"] = at, self.raw[:, slot]
        if u["direct"]:
            u["ready"], u["slot"] = arrived, slot
            return
        c = self.nconv % self.CONV
        self.nconv += 1
        src = self.raw[0:p, slot, 0:n, 0:at]
        hi, lo = self.hi[0:p, c, 0:n, 0:at], self.lo[0:p, c, 0:n, 0:at]
        a = self.act.op(self.nc.scalar.activation, [arrived, self.conv_free[c]], hi, src, ACT.Copy)
        v = self.dve.op(self.nc.vector.tensor_tensor, a, lo, src, hi.bitcast(F32), ALU.subtract)
        self.raw_free[slot] = [a, v]
        u["ready"], u["slot"], u["hi"], u["lo"] = v, c, self.hi[:, c], self.lo[:, c]

    def fetch(self, i):
        while self.prepared < min(len(self.units), i + 1 + self.AHEAD):
            self._prepare(self.prepared)
            self.prepared += 1
        return self.units[i]

    def done(self, u, mark):
        if u["direct"]:
            self.raw_free[u["slot"]] = mark
        else:
            self.conv_free[u["slot"]] = mark


def interleave(lanes, width):
    lanes, live, free = list(lanes), [], list(range(width))
    while lanes or live:
        while lanes and free:
            lane = free.pop(0)
            live.append((lanes.pop(0)(lane), lane))
        for g, lane in list(live):
            try:
                next(g)
            except StopIteration:
                live.remove((g, lane))
                free.append(lane)


def program(nc, I, K, out):
    with ExitStack() as ctx:
        def sb(name, shape, dt=F32, on=None):
            return (on or ctx).enter_context(nc.sbuf_tensor(name, shape, dt))

        def dma_counter(name):
            return [ctx.enter_context(nc.semaphore(name)), 0]

        act, dve, pool, pe, sp = (Queue(ctx.enter_context(nc.semaphore(f"{n}_done")))
                                  for n in ("act", "dve", "pool", "pe", "sp"))
        c_const, c_pack, c_x, c_ctx, c_out, c_lam, c_mask = (dma_counter(n) for n in (
            "consts_in", "packs_in", "x_in", "ctx_in", "out_stored", "lambda_in", "masks_in"))
        c_ring = [dma_counter(f"weights_in{i}") for i in range(Weights.RAW)]
        c_bias = [dma_counter(f"bias_in{i}") for i in range(3)]

        def activation(dst, src, func, after, **kw):
            return act.op(nc.scalar.activation, after, dst, src, func, **kw)

        def tt(dst, a, b, op, after, q=None):
            q = q or dve
            f = nc.gpsimd.tensor_tensor if q is pool else nc.vector.tensor_tensor
            return q.op(f, after, dst, a, b, op)

        def stt(dst, a, scalar, b, op0, op1, after):
            return dve.op(nc.vector.scalar_tensor_tensor, after, out=dst, in0=a, scalar=scalar,
                          in1=b, op0=op0, op1=op1)

        def ts(dst, a, s1, s2, op0, op1, after):
            if s2 is None:
                return dve.op(nc.vector.tensor_scalar, after, dst, a, s1, None, op0)
            return dve.op(nc.vector.tensor_scalar, after, dst, a, s1, s2, op0, op1)

        def copy(dst, src, after, q=None):
            q = q or dve
            if q is act:
                return activation(dst, src, ACT.Copy, after)
            return q.op(nc.gpsimd.tensor_copy if q is pool else nc.vector.tensor_copy, after, dst, src)

        def mm(dst, lhsT, rhs, after, start=True, stop=True, mark=True, **kw):
            return (pe.op if mark else pe.quiet)(nc.tensor.matmul, after, dst, lhsT, rhs,
                                                 start=start, stop=stop, **kw)

        def turn(dst, src, after, mark=True):
            n = src.shape[0]
            return (pe.op if mark else pe.quiet)(nc.tensor.transpose, after, dst, src, ident[0:n, 0:n])

        def load(dst, src, counter, *after):
            return sp.dma(nc.sync.dma_start, dst, src, counter, *after)

        ps = ctx.enter_context(nc.psum_tensor("banks", [P, 8, T], F32))
        bank_free = [None] * 8
        next_bank = [0]

        def take_bank():
            next_bank[0] = (next_bank[0] + 1) % 8
            return next_bank[0]

        ring_raw = sb("weights_raw", [P, Weights.RAW, 2, 512])
        ring_hi = sb("weights_hi", [P, Weights.CONV, 2, 512], F32R)
        ring_lo = sb("weights_lo", [P, Weights.CONV, 2, 512], F32R)
        x = sb("x_turned", [P, KC, T])
        ident = sb("ident", [P, P])
        ones = sb("ones", [P, P])
        headsum = sb("headsum", [P, P])
        vecs = sb("vectors", [P, 256])
        rstd = sb("rstd", [P, T])
        sq = sb("squares", [P, 2, T])
        sq_sum = sb("squares_sum", [P, T])
        eps = sb("eps", [P, 4])
        W = Weights(nc, ring_raw, ring_hi, ring_lo, c_ring, sp, act, dve)
        column = {}
        for base, pack in ((0, PACK1), (P, PACK2)):
            for name, n in pack:
                column[name] = base
                base += n

        def vec(name, k=0):
            return vecs[:, column[name] + k:column[name] + k + 1]

        def columns(w, c0, c1):
            return lambda r0, n, part: w[r0:r0 + n, c0:c1].rearrange("(k p) n -> p k n", p=part)

        def dense(w, step=512, c0=0, c1=None, **kw):
            c1 = c1 or w.shape[1]
            return W.plan(w.shape[0], [[columns(w, c, min(c + step, c1))] for c in range(c0, c1, step)], **kw)

        def ffn_plan(l, s):
            w_in, w_out = I["ffn_w_in"][l, s], I["ffn_w_out"][l, s]
            parts = []
            for f0, f1 in ((0, KF // 2 + 1), (KF // 2 + 1, KF)):
                gate_up = W.plan(C, [[columns(w_in, f * P, (f + 2) * P), columns(w_in, F + f * P, F + (f + 2) * P)]
                                     for f in range(f0, f1, 2)])
                parts.append((gate_up, dense(w_out[f0 * P:f1 * P, :])))
            return parts

        w_in2, w_ukv, w_uq = I["w_in_2"][0], I["w_ukv_2"][0], I["w_uq_2"][0]
        span, at = {}, 0
        for n, w in (("ckv", 128), ("kr", 32), ("kb", 512), ("vb", 512), ("cq", 256), ("za", 512),
                     ("qb", 512), ("zb", 512), ("ga", 1024), ("gb", 1024)):
            span[n] = (at, at + w)
            at += w

        def w_in_part(n):
            return dense(w_in2, c0=span[n][0], c1=span[n][1])

        layer = {"ffn00": ffn_plan(0, 0)}
        for n in ("w1", "a1", "g1"):
            layer[n] = dense(I[f"rwkv_{n}"][0], direct=True)
        for s in range(3):
            layer["rkv", s] = dense(I["rwkv_w_rkv"][0, s])
        for m in range(KC):
            for n in ("w2", "a2", "g2"):
                layer[n, m] = dense(I[f"rwkv_{n}"][0], c0=m * P, c1=m * P + P, direct=True, nk=1)
        layer["rwkv_o"] = dense(I["rwkv_w_o"][0])
        layer["ffn01"] = ffn_plan(0, 1)
        layer["kv"] = dense(I["w_kv"])
        layer["ffn10"] = ffn_plan(1, 0)
        layer["q"] = dense(I["diff_w_q"][0])
        layer["diff_o"] = dense(I["diff_w_o"][0])
        layer["ffn11"] = ffn_plan(1, 1)
        layer["mod"] = dense(I["w_mod_2"][0], direct=True)
        layer["ckv"] = W.plan(C, [[columns(w_in2, 0, 160)]])
        layer["uk"] = dense(w_ukv)
        layer["uv"] = W.plan(P, [[lambda r0, n, part: w_ukv.rearrange(
            "(k p) (h c) -> p k h c", p=part, c=P)[:, :, :, NOPE:P]]])
        layer["cq"] = w_in_part("cq")
        layer["uq"] = dense(w_uq, step=4 * QK)
        for n in ("kb", "vb", "qb", "za", "ga"):
            layer[n] = w_in_part(n)
        layer["w_oa"] = dense(I["w_oa_2"][0])
        layer["zb"] = w_in_part("zb")
        layer["gb"] = w_in_part("gb")
        layer["w_ob"] = dense(I["w_ob_2"][0])
        layer["w_out"] = dense(I["w_out_2"][0])

        def linear(blocks, operand, evac, natural=False, tiles=None, extra=None):
            for bi, ids in enumerate(blocks):
                width = W.fetch(ids[0])["width"]
                jobs = []
                for opnd, ev in [(operand, evac)] + ([extra] if extra else []):
                    ntok = opnd(0)[0].shape[1]
                    spans = ([(c, P) for c in range(0, ntok, P)] if natural else
                             tiles or [(c, P) for c in range(0, width, P)])
                    jobs += [(opnd, ev, i, c0, m, take_bank(), ntok) for i, (c0, m) in enumerate(spans)]
                for uid in ids:
                    u = W.fetch(uid)
                    for opnd, ev, i, c0, m, b, ntok in jobs:
                        for kk in range(u["nk"]):
                            xh, xl, ready = opnd(u["k0"] + kk)
                            first, last = u["k0"] + kk == 0, uid == ids[-1] and kk == u["nk"] - 1
                            if natural:
                                o = ps[:, b, 0:width]
                                wh, wl = u["hi"][:, kk, 0:width], u["lo"][:, kk, 0:width]
                                xh, xl = xh[:, c0:c0 + m], xl[:, c0:c0 + m]
                                terms = ((xh, wh), (xh, wl), (xl, wh))
                            else:
                                o = ps[0:m, b, 0:ntok]
                                wh, wl = u["hi"][:, kk, c0:c0 + m], u["lo"][:, kk, c0:c0 + m]
                                terms = ((wh, xh), (wh, xl), (wl, xh))
                            for t, (l, r) in enumerate(terms):
                                mark = mm(o, l, r, [u["ready"], ready, bank_free[b] if first else None],
                                          start=first and t == 0, stop=last and t == 2,
                                          mark=t == 2 and kk == u["nk"] - 1)
                        if uid == ids[-1]:
                            bank_free[b] = ev(bi, i, b, mark)
                    W.done(u, mark)

        def split(hi, lo, src, after, scale=None):
            if scale is None:
                h = activation(hi, src, ACT.Copy, after)
                return [h, tt(lo, src, hi.bitcast(F32), ALU.subtract, h)]
            h = activation(hi, src, ACT.Copy, after, scale=scale)
            return [h, stt(lo, src, scale, hi.bitcast(F32), ALU.mult, ALU.subtract, h)]

        class Operand:

            def __init__(self, name, tiles, on, width=T):
                self.hi = sb(f"{name}_hi", [P, tiles, width], F32R, on=on)
                self.lo = sb(f"{name}_lo", [P, tiles, width], F32R, on=on)
                self.marks, self.used = [None] * tiles, None

            def put(self, k, src, after, scale=None):
                self.marks[k] = split(self.hi[:, k], self.lo[:, k], src, [after, self.used], scale)
                return self.marks[k]

            def __call__(self, k):
                return self.hi[:, k], self.lo[:, k], self.marks[k]

        def fence():
            marks = [q.now() for q in (act, dve, pool, pe)]
            for q in (act, dve, pool, pe, sp):
                q.wait(*marks)

        def inv_sqrt(dst, src, scale, eps_col, after):
            n = dst.shape[0]
            r = activation(dst, src, ACT.Sqrt, after, bias=eps[0:n, eps_col:eps_col + 1], scale=scale)
            return dve.op(nc.vector.reciprocal, r, dst, dst)

        EPS_NORM, EPS_RWKV, EPS_SUBLN, EPS_NONE = range(4)
        x_marks = [None] * KC
        state = {"sum_used": None, "rstd": None}
        sq_used = [None, None]

        def rms(tiles, after=None, dst=None, channels=C):
            dst = rstd[:, :] if dst is None else dst
            w = tiles[0][0].shape[1]
            for k, (t, m) in enumerate(tiles):
                a = activation(sq[:, k % 2, 0:w], t, ACT.Square, [m, sq_used[k % 2]])
                if k == 0:
                    s = copy(sq_sum[:, 0:w], sq[:, 0, 0:w], [a, state["sum_used"]])
                else:
                    s = tt(sq_sum[:, 0:w], sq_sum[:, 0:w], sq[:, k % 2, 0:w], ALU.add, [a, s])
                sq_used[k % 2] = s
            b = take_bank()
            p = mm(ps[:, b, 0:w], ones[:, :], sq_sum[:, 0:w], [s, consts, bank_free[b]])
            state["sum_used"] = p
            r = inv_sqrt(dst, ps[:, b, 0:w], 1.0 / channels, EPS_NORM, [p, after])
            bank_free[b] = r
            return r

        def rms_x():
            state["rstd"] = rms([(x[:, k], x_marks[k]) for k in range(KC)])

        def scaled_x(opnd, gain, k0=0):
            for k in range(KC):
                opnd.put(k, x[:, k], x_marks[k], vec(gain, k0 + k))

        def head_norm(dst, gain, tmp, after):
            a = activation(sq[:, 0, :], dst, ACT.Square, [after, sq_used[0]])
            b = take_bank()
            p = mm(ps[:, b], headsum[:, :], sq[:, 0], [a, bank_free[b]])
            sq_used[0] = p
            r = inv_sqrt(tmp, ps[:, b], 1.0 / HEAD, EPS_NORM, [p])
            bank_free[b] = r
            return stt(dst, dst, gain, tmp, ALU.mult, ALU.mult, r)

        load(ident[:, :], K["ident"], c_const)
        m_const = load(headsum[:, :], K["headsum"], c_const)
        m = pool.op(nc.gpsimd.memset, None, ones[:, :], 1.0)
        for i, v in enumerate((1e-6, 64e-5, 1e-5, 0.0)):
            m = pool.op(nc.gpsimd.memset, None, eps[:, i:i + 1], v)
        consts = [m_const, m]
        with ExitStack() as ph:
            packs = sb("packs", [P, 2, P], on=ph)
            x_in = sb("x_in", [P, TB, C], on=ph)
            m_x = load(x_in[:, :, :], I["x"][0].rearrange("(b p) c -> p b c", p=P), c_x)
            clear = dve.op(nc.vector.memset, None, packs[:, :, :], 0.0)
            for i, pack in enumerate((PACK1, PACK2)):
                r = 0
                for name, n in pack:
                    if name in ("diff_q_norm", "k_norm"):
                        for h in range(2):
                            m_pack = load(packs[r:r + 1, i, h * HEAD:(h + 1) * HEAD], K["flat_" + name],
                                          c_pack, clear)
                    else:
                        m_pack = load(packs[r:r + n, i, :], K["flat_" + name], c_pack, clear)
                    r += n
            b = take_bank()
            for i in range(2):
                m = turn(ps[:, b, i * P:(i + 1) * P], packs[:, i], [m_pack, consts])
            m_vec = copy(vecs[:, :], ps[:, b, 0:2 * P], m)
            bank_free[b] = m_vec
            for k in range(KC):
                b = take_bank()
                for tb in range(TB):
                    m = turn(ps[:, b, tb * P:(tb + 1) * P], x_in[:, tb, k * P:(k + 1) * P],
                             [m_x, consts, bank_free[b]])
                x_marks[k] = bank_free[b] = copy(x[:, k], ps[:, b], m)
        for q in (act, dve, pool, pe):
            q.wait(m_vec, consts)
        fence()

        def ffn(parts, tag, k0):
            with ExitStack() as ph:
                h = Operand(f"h_{tag}", KC, ph)
                hidden = Operand(f"hidden_{tag}", KF // 2 + 1, ph)
                tmp = sb(f"ffn_tmp_{tag}", [P, 3, 3, T], on=ph)
                tmp_used, gate_mark = [None] * 3, [None] * 3
                scaled_x(h, "ffn_norm", k0)
                rms_x()

                def gate_up(bi, i, b, mark):
                    s = (2 * bi + i % 2) % 3
                    m = tt(tmp[:, s, i // 2], ps[:, b], rstd[:, :], ALU.mult, [mark, state["rstd"], tmp_used[s]])
                    if i < 2:
                        gate_mark[s] = activation(tmp[:, s, 0], tmp[:, s, 0], ACT.Silu, m)
                        return m
                    f = 2 * bi + i - 2
                    g = tt(tmp[:, s, 2], tmp[:, s, 0], tmp[:, s, 1], ALU.mult, [gate_mark[s], m])
                    tmp_used[s] = hidden.put(f, tmp[:, s, 2], g)
                    return m

                def add(bi, i, b, mark):
                    k = 4 * bi + i
                    x_marks[k] = stt(x[:, k], ps[:, b], 0.5, x[:, k], ALU.mult, ALU.add, [mark, x_marks[k], x_read])
                    return x_marks[k]

                x_read = act.now()
                for up, down in parts:
                    linear(up, h, gate_up)
                    h.used = pe.now()
                    linear(down, hidden, add)
                    hidden.used = pe.now()
            fence()

        ffn(layer["ffn00"], "ffn00", 0)

        MIX_R, MIX_K, MIX_V, MIX_W, MIX_A, MIX_G = range(6)
        with ExitStack() as ph:
            rkv = [sb(n, [P, KC, T], on=ph) for n in ("r", "k", "v")]
            lora = [sb(n, [P, T], on=ph) for n in ("lora_w", "lora_a", "lora_g", "lora_g_rest")]
            rms_x()
            with ExitStack() as ph2:
                h = sb("h_shifted", [P, KC, T + 1], on=ph2)
                dx = sb("dx", [P, KC, T], on=ph2)
                mixed = sb("mixed", [P, 4, T], on=ph2)
                opnd = Operand("mix", KC, ph2)
                first = dve.op(nc.vector.memset, None, h[:, :, 0:1], 0.0)
                dx_marks = []
                for k in range(KC):
                    m = stt(h[:, k, 1:T + 1], x[:, k], vec("mix_norm", k), rstd[:, :], ALU.mult, ALU.mult,
                            [state["rstd"], x_marks[k]])
                    dx_marks.append(tt(dx[:, k], h[:, k, 0:T], h[:, k, 1:T + 1], ALU.subtract, [m, first]))
                mixed_used = [None] * 4

                def mix(k, which, slot):
                    return stt(mixed[:, slot], dx[:, k], vec("rwkv_mu", which * KC + k), h[:, k, 1:T + 1],
                               ALU.mult, ALU.add, [dx_marks[k], mixed_used[slot]])

                for n, which, outs in (("w1", MIX_W, ((0, 64, lora[0], ACT.Tanh),)),
                                       ("a1", MIX_A, ((0, 64, lora[1], ACT.Copy),)),
                                       ("g1", MIX_G, ((0, 128, lora[2], ACT.Sigmoid), (128, 160, lora[3], ACT.Sigmoid)))):
                    banks = [take_bank() for _ in outs]
                    for uid in layer[n][0]:
                        u = W.fetch(uid)
                        for kk in range(u["nk"]):
                            k = u["k0"] + kk
                            m = mix(k, which, k % 4)
                            for b, (c0, c1, _, _) in zip(banks, outs):
                                mark = mm(ps[0:c1 - c0, b], u["raw"][:, kk, c0:c1], mixed[:, k % 4],
                                          [m, u["ready"], bank_free[b] if k == 0 else None],
                                          start=k == 0, stop=k == KC - 1)
                            mixed_used[k % 4] = mark
                        W.done(u, mark)
                    for b, (c0, c1, dst, func) in zip(banks, outs):
                        bank_free[b] = activation(dst[0:c1 - c0, :], ps[0:c1 - c0, b], func, mark)
                lora_mark = act.now()
                for s in range(3):
                    for k in range(KC):
                        mixed_used[k % 4] = opnd.put(k, mixed[:, k % 4], mix(k, s, k % 4))

                    def keep(bi, i, b, mark, s=s):
                        return copy(rkv[s][:, 4 * bi + i], ps[:, b], mark, q=act)
                    linear(layer["rkv", s], opnd, keep)
                    opnd.used = pe.now()
            fence()

            with ExitStack() as ph2:
                masks = sb("masks", [P, 2, P], on=ph2)
                seed = sb("seed_masks", [P, 2, P], on=ph2)
                level = sb("level_masks", [P, 5, P], on=ph2)
                center = sb("center", [P, P], on=ph2)
                run = sb("scan_reset", [P, T], on=ph2)
                tmp = sb("wkv_tmp", [P, 8, T], on=ph2)
                ar = sb("a_r_turned", [P, TB, 2, P], on=ph2)
                bt = sb("b_turned", [P, T], on=ph2)
                kt = sb("k_turned", [P, T], on=ph2)
                av = sb("a_nv", [P, 8, P], on=ph2)
                bn = sb("b_natural", [P, TB, P], on=ph2)
                kn = sb("k_natural", [P, TB, P], on=ph2)
                vn = sb("v_natural", [P, TB, P], on=ph2)
                mq = sb("m_q", [P, 8, 2, P], on=ph2)
                nq = sb("n_q", [P, 8, 2, P], on=ph2)
                inv = sb("inverse", [P, 8, P], on=ph2)
                inv_t = sb("inverse_turned", [P, 8, P], on=ph2)
                xw = sb("x_or_w", [P, 8, P], on=ph2)
                zt = sb("z_turned", [P, T], on=ph2)
                m_masks = None
                for dst, n in ((masks, "masks"), (seed, "seed"), (level, "level")):
                    m_masks = load(dst[:, :, :], K[n].rearrange("p (a b) -> p a b", b=P), c_mask)
                for dst, n in ((center, "center"), (run, "run")):
                    m_masks = load(dst[:, :], K[n], c_mask)
                for q in (dve, pe, pool):
                    q.wait(m_masks)
                gbd, hbd, sbd = nq[:, :, 0, :], mq[:, :, 0, :], inv
                chunks = lambda a: a.rearrange("p (c t) -> p c t", t=CHUNK)
                blocks = lambda a: a.rearrange("p (b t) -> p b t", t=P)
                r_all, k_all, v_all = rkv

                def small(name, m, rows_list):
                    b = take_bank()
                    ids = layer[name, m][0]
                    for j, (uid, rhs) in enumerate(zip(ids, rows_list)):
                        u = W.fetch(uid)
                        mark = mm(ps[:, b], u["raw"][0:u["part"], 0, 0:P], rhs[0:u["part"], :],
                                  [u["ready"], lora_mark, bank_free[b]], start=j == 0, stop=j == len(ids) - 1)
                        W.done(u, mark)
                    return b, mark

                def keep_bank(b, mark):
                    bank_free[b] = mark
                    return mark

                prev = {"pe": None, "act": None, "dve": None, "pool": None}
                y_marks = [None] * KC
                for m in range(KC):
                    t = [tmp[:, i] for i in range(8)]
                    r, k, v = r_all[:, m], k_all[:, m], v_all[:, m]
                    for q in (act, dve, pool):
                        q.wait(pe.now(), act.now(), dve.now(), pool.now())
                    b, mk = small("w2", m, [lora[0]])
                    z = keep_bank(b, activation(t[0], ps[:, b], ACT.Sigmoid, mk, bias=vec("rwkv_w0", m)))
                    b, mk = small("a2", m, [lora[1]])
                    a = keep_bank(b, activation(t[4], ps[:, b], ACT.Sigmoid, mk, bias=vec("rwkv_a0", m)))
                    lw = ts(t[0], t[0], -math.exp(-0.5), None, ALU.mult, None, z)
                    cs = dve.op(nc.vector.tensor_tensor_scan, lw, t[1], run[:, :], t[0], 0.0, ALU.mult, ALU.add)
                    cl = tt(t[6], t[1], t[0], ALU.subtract, cs)
                    ea = activation(t[6], t[6], ACT.Exp, cl)
                    ep = activation(t[2], t[1], ACT.Exp, cs)
                    en = activation(t[3], t[1], ACT.Exp, cs, scale=-1.0)
                    s = activation(t[7], k, ACT.Square, None, scale=vec("rwkv_k_k", m))
                    b = take_bank()
                    mk = mm(ps[:, b], headsum[:, :], t[7], [s, bank_free[b]])
                    n2 = keep_bank(b, ts(t[7], ps[:, b], 1e-24, None, ALU.max, None, mk))
                    n2 = inv_sqrt(t[7], t[7], 1.0, EPS_NONE, n2)
                    kk = stt(t[5], k, vec("rwkv_k_k", m), t[7], ALU.mult, ALU.mult, n2)
                    m_a = stt(ar[:, :, 0, :], blocks(t[5]), -1.0, blocks(t[6]), ALU.mult, ALU.mult, [kk, ea])
                    ka = tt(t[7], t[5], t[4], ALU.mult, [kk, a])
                    m_b = tt(bt[:, :], t[7], t[3], ALU.mult, [ka, en])
                    am = ts(t[4], t[4], -1.0, vec("rwkv_k_a", m), ALU.add, ALU.mult, ka)
                    k2 = stt(t[4], t[4], 1.0, k, ALU.add, ALU.mult, am)
                    m_k = tt(kt[:, :], t[4], t[3], ALU.mult, k2)
                    m_r = tt(ar[:, :, 1, :], blocks(r), blocks(t[2]), ALU.mult, ep)
                    bonus = stt(t[6], r, vec("rwkv_r_k", m), t[4], ALU.mult, ALU.mult, [k2, m_a])
                    last = chunks(t[2])[:, :, CHUNK - 1:CHUNK]
                    b2 = tt(chunks(t[0]), chunks(bt[:, :]), last.broadcast_to([P, NCH, CHUNK]), ALU.mult, [m_b, cl])
                    k3 = tt(chunks(t[1]), chunks(kt[:, :]), last.broadcast_to([P, NCH, CHUNK]), ALU.mult, [m_k, ep, en])
                    nat = []
                    for src, mark, dst in ((ar[:, :, 0, :], m_a, av), (blocks(t[0]), b2, bn),
                                           (blocks(t[1]), k3, kn), (blocks(v), None, vn)):
                        b = take_bank()
                        for tb in range(TB):
                            mk = turn(ps[:, b, tb * P:(tb + 1) * P], src[:, tb], [mark, bank_free[b]])
                        if dst is av:
                            for e in range(2):
                                o = copy(av[:, 4 * e:4 * e + 4, 0:HEAD],
                                         blocks(ps[:, b])[:, :, e * HEAD:(e + 1) * HEAD], mk, q=act)
                        else:
                            o = copy(dst[:, :, :], blocks(ps[:, b]), mk, q=act)
                        nat.append(keep_bank(b, o))
                    def pairs(lhs, dst, mark):
                        out_marks = []
                        for g in range(4):
                            b = take_bank()
                            for j in range(2):
                                p = 2 * g + j
                                e, tb = p // 4, p % 4
                                h0 = e * HEAD
                                mk = mm(ps[:, b, j * 256:(j + 1) * 256], lhs[h0:h0 + HEAD, tb * P:(tb + 1) * P],
                                        ar[h0:h0 + HEAD, tb, :, :], [mark, m_a, m_r, bank_free[b]])
                            out_marks.append(keep_bank(b, tt(
                                dst[:, 2 * g:2 * g + 2], ps[:, b].rearrange("p (q a t) -> p q a t", q=2, a=2),
                                masks[:, :, :].unsqueeze(1).broadcast_to([P, 2, 2, P]), ALU.mult, mk)))
                        return out_marks
                    m_mq = pairs(bt, mq, m_b)
                    i4 = ident[:, :].unsqueeze(1).broadcast_to([P, 4, P])
                    m_inv, m_invt = [], []
                    for e in range(2):
                        b = take_bank()
                        for tb in range(TB):
                            h0 = e * HEAD
                            mk = mm(ps[:, b, tb * P:(tb + 1) * P], ar[h0:h0 + HEAD, tb, 0, :],
                                    bt[h0:h0 + HEAD, tb * P:(tb + 1) * P], [m_a, m_b, bank_free[b]])
                        o = keep_bank(b, tt(inv[:, 4 * e:4 * e + 4], blocks(ps[:, b]),
                                            seed[:, 0].unsqueeze(1).broadcast_to([P, 4, P]), ALU.mult, mk))
                        m_inv.append(tt(inv[:, 4 * e:4 * e + 4], inv[:, 4 * e:4 * e + 4], i4, ALU.add, o))
                        o = tt(inv_t[:, 4 * e:4 * e + 4], mq[:, 4 * e:4 * e + 4, 0, :],
                               seed[:, 1].unsqueeze(1).broadcast_to([P, 4, P]), ALU.mult, m_mq)
                        m_invt.append(tt(inv_t[:, 4 * e:4 * e + 4], inv_t[:, 4 * e:4 * e + 4], i4, ALU.add, o))
                    m_nq = pairs(kt, nq, m_k)
                    for lv in range(5):
                        m_x = []
                        for e in range(2):
                            b = take_bank()
                            for tb in range(TB):
                                p = 4 * e + tb
                                mk = mm(ps[:, b, tb * P:(tb + 1) * P], mq[:, p, 0, :], inv[:, p],
                                        [m_mq, m_inv[e], bank_free[b]])
                            m_x.append(keep_bank(b, tt(xw[:, 4 * e:4 * e + 4], blocks(ps[:, b]),
                                                       level[:, lv].unsqueeze(1).broadcast_to([P, 4, P]),
                                                       ALU.mult, [mk, pe.now()])))
                        for e in range(2):
                            for turned in (True, False) if lv < 4 else (True,):
                                b = take_bank()
                                for tb in range(TB):
                                    p = 4 * e + tb
                                    l, rr = (xw[:, p], inv_t[:, p]) if turned else (inv_t[:, p], xw[:, p])
                                    mk = mm(ps[:, b, tb * P:(tb + 1) * P], l, rr,
                                            [m_x[e], m_invt[e], bank_free[b]])
                                if turned:
                                    held = (b, mk)
                                else:
                                    m_inv[e] = keep_bank(b, tt(inv[:, 4 * e:4 * e + 4], inv[:, 4 * e:4 * e + 4],
                                                               blocks(ps[:, b]), ALU.add, [mk, m_inv[e]]))
                            b, _ = held
                            m_invt[e] = keep_bank(b, tt(inv_t[:, 4 * e:4 * e + 4], inv_t[:, 4 * e:4 * e + 4],
                                                        blocks(ps[:, b]), ALU.add, [pe.now(), m_invt[e]]))
                    b = take_bank()
                    for p in range(8):
                        e, tb = p // 4, p % 4
                        mk = mm(ps[:, b, p * HEAD:(p + 1) * HEAD], nq[:, p, 0, :],
                                vn[:, tb, e * HEAD:(e + 1) * HEAD], [m_nq, nat[3], bank_free[b]])
                    m_nv = keep_bank(b, copy(av[:, :, HEAD:P], ps[:, b].rearrange("p (q v) -> p q v", q=8), mk, q=act))
                    m_w = []
                    for e in range(2):
                        b = take_bank()
                        for tb in range(TB):
                            p = 4 * e + tb
                            mk = mm(ps[:, b, tb * P:(tb + 1) * P], inv_t[:, p], av[:, p],
                                    [m_invt[e], m_nv, nat[0], bank_free[b]])
                        m_w.append(keep_bank(b, copy(xw[:, 4 * e:4 * e + 4], blocks(ps[:, b]), mk, q=act)))
                    clear = []
                    for a_ in (gbd, hbd):
                        for e in range(2):
                            clear.append(pool.op(nc.gpsimd.memset, [mk], a_[e * HEAD:(e + 1) * HEAD, :,
                                                 (1 - e) * HEAD:(2 - e) * HEAD], 0.0))
                    m_gh = []
                    for e in range(2):
                        h0 = e * HEAD
                        m_gh.append(tt(gbd[h0:h0 + HEAD, :, h0:h0 + HEAD],
                                       ident[h0:h0 + HEAD, h0:h0 + HEAD].unsqueeze(1).broadcast_to([HEAD, NCH, HEAD]),
                                       last[h0:h0 + HEAD].broadcast_to([HEAD, NCH, HEAD]), ALU.mult, [mk]))
                    for j in range(2):
                        b = take_bank()
                        j0 = j * HEAD
                        for tb in range(TB):
                            for e in range(2):
                                h0, p = e * HEAD, 4 * e + tb
                                mm(ps[h0:h0 + HEAD, b, tb * HEAD:(tb + 1) * HEAD], xw[j0:j0 + HEAD, p, 0:HEAD],
                                   bn[j0:j0 + HEAD, tb, h0:h0 + HEAD], [m_w, nat[1], bank_free[b]])
                        for tb in range(TB):
                            for e in range(2):
                                h0, p = e * HEAD, 4 * e + tb
                                o = ps[h0:h0 + HEAD, b, 256 + tb * HEAD:256 + (tb + 1) * HEAD]
                                mm(o, bn[j0:j0 + HEAD, tb, h0:h0 + HEAD], xw[j0:j0 + HEAD, p, HEAD:P], None,
                                   stop=False)
                                mk = mm(o, kn[j0:j0 + HEAD, tb, h0:h0 + HEAD], vn[j0:j0 + HEAD, tb, h0:h0 + HEAD],
                                        [nat[2], nat[3]], start=False)
                        for e in range(2):
                            h0 = e * HEAD
                            gv = gbd[h0:h0 + HEAD].rearrange("p (b j) n -> p j b n", j=2)[:, j, :, h0:h0 + HEAD]
                            hv = hbd[h0:h0 + HEAD].rearrange("p (b j) n -> p j b n", j=2)[:, j, :, h0:h0 + HEAD]
                            pv = ps[h0:h0 + HEAD, b].rearrange("p (g b n) -> p g b n", g=2, b=TB)
                            m_gh.append(tt(gv, pv[:, 0], gv, ALU.add, [mk, m_gh[e]]))
                            m_gh.append(copy(hv, pv[:, 1], mk))
                        keep_bank(b, m_gh[-1])
                    b = take_bank()
                    for p in range(8):
                        e, tb = p // 4, p % 4
                        mk = mm(ps[e * HEAD:(e + 1) * HEAD, b, tb * P:(tb + 1) * P], xw[:, p, 0:HEAD],
                                mq[:, p, 1, :], [m_w, bank_free[b]])
                    m_z = keep_bank(b, tt(blocks(zt[:, :]), blocks(ps[:, b]), ar[:, :, 1, :], ALU.add, mk))
                    states = [None, copy(sbd[:, 1], hbd[:, 0], [m_gh, clear, pe.now()])]
                    for c in range(1, NCH - 1):
                        b = take_bank()
                        mk = mm(ps[:, b, 0:P], gbd[:, c], sbd[:, c], [states[c], m_gh, clear, bank_free[b]])
                        states.append(keep_bank(b, tt(sbd[:, c + 1], ps[:, b, 0:P], hbd[:, c], ALU.add, mk)))
                    b = take_bank()
                    for tb in range(TB):
                        for e in range(2):
                            p = 4 * e + tb
                            o = ps[e * HEAD:(e + 1) * HEAD, b, tb * P:(tb + 1) * P]
                            mm(o, xw[:, p, HEAD:P], mq[:, p, 1, :], bank_free[b], stop=False, skip_group_check=True)
                            mm(o, vn[:, tb, e * HEAD:(e + 1) * HEAD], nq[:, p, 1, :], None, start=False,
                               stop=False, skip_group_check=True)
                        for c in (2 * tb, 2 * tb + 1):
                            if c:
                                mk = mm(ps[:, b, c * CHUNK:(c + 1) * CHUNK], sbd[:, c], zt[:, c * CHUNK:(c + 1) * CHUNK],
                                        [states[c], m_z], start=False, stop=c % 2 == 1, skip_group_check=True)
                    y = keep_bank(b, copy(t[0], ps[:, b], mk, q=act))
                    b = take_bank()
                    mk = mm(ps[:, b], headsum[:, :], t[6], [bonus, bank_free[b]])
                    m_bonus = keep_bank(b, tt(t[6], ps[:, b], v, ALU.mult, mk))
                    b = take_bank()
                    mk = mm(ps[:, b], center[:, :], t[0], [y, bank_free[b]])
                    yc = keep_bank(b, copy(t[1], ps[:, b], mk, q=act))
                    s = activation(t[2], t[1], ACT.Square, yc)
                    b = take_bank()
                    mk = mm(ps[:, b], headsum[:, :], t[2], [s, bank_free[b]])
                    iv = keep_bank(b, inv_sqrt(t[3], ps[:, b], 1.0 / HEAD, EPS_RWKV, mk))
                    yn = tt(t[1], t[1], t[3], ALU.mult, iv)
                    yn = ts(t[1], t[1], vec("rwkv_ln_g", m), vec("rwkv_ln_b", m), ALU.mult, ALU.add, yn)
                    yn = tt(t[1], t[1], t[6], ALU.add, [yn, m_bonus])
                    b, mk = small("g2", m, [lora[2], lora[3]])
                    y_marks[m] = keep_bank(b, tt(r, t[1], ps[:, b], ALU.mult, [mk, yn]))
            fence()
            with ExitStack() as ph2:
                opnd = Operand("wkv_out", KC, ph2)
                for m in range(KC):
                    opnd.put(m, r_all[:, m], y_marks[m])

                def add_x(bi, i, b, mark):
                    k = 4 * bi + i
                    x_marks[k] = tt(x[:, k], ps[:, b], x[:, k], ALU.add, [mark, x_marks[k], act.now()])
                    return x_marks[k]
                linear(layer["rwkv_o"], opnd, add_x)
        fence()

        ffn(layer["ffn01"], "ffn01", KC)

        with ExitStack() as ph:
            kT = sb("diff_keys", [P, KC, T], on=ph)
            V = sb("diff_values", [P, TB, C], on=ph)
            with ExitStack() as ph2:
                h = Operand("kv_in", KC, ph2)
                tmp = sb("kv_tmp", [P, T], on=ph2)
                rcol = sb("rstd_column", [P, TB], on=ph2)
                scaled_x(h, "kv_norm")
                rms_x()
                b = take_bank()
                for tb in range(TB):
                    mk = mm(ps[:, b, tb:tb + 1], rstd[0:1, tb * P:(tb + 1) * P], ones[0:1, 0:1],
                            [state["rstd"], bank_free[b]])
                m_rcol = bank_free[b] = copy(rcol[:, :], ps[:, b, 0:TB], mk)

                def keys(bi, i, b, mark):
                    k = 4 * bi + i
                    m = tt(kT[:, k], ps[:, b], rstd[:, :], ALU.mult, [mark, state["rstd"]])
                    head_norm(kT[:, k], vec("k_norm"), tmp[:, :], m)
                    return m

                def values(bi, i, b, mark):
                    return ts(V[:, i, bi * T:(bi + 1) * T], ps[:, b], rcol[:, i:i + 1], None, ALU.mult, None,
                              [mark, m_rcol])
                linear(layer["kv"][0:2], h, keys)
                linear(layer["kv"][2:4], h, values, natural=True)
            fence()
            kv_marks = [dve.now()]

            ffn(layer["ffn10"], "ffn10", 2 * KC)

            LAM_INIT = 0.8 - 0.6 * math.exp(-0.3 * 1)
            with ExitStack() as ph2:
                q = sb("diff_queries", [P, KC, T], on=ph2)
                with ExitStack() as ph3:
                    h = Operand("q_in", KC, ph3)
                    tmp = sb("q_tmp", [P, T], on=ph3)
                    scaled_x(h, "mix_norm", KC)
                    rms_x()

                    def queries(bi, i, b, mark):
                        k = 4 * bi + i
                        m = tt(q[:, k], ps[:, b], rstd[:, :], ALU.mult, [mark, state["rstd"]])
                        head_norm(q[:, k], vec("diff_q_norm"), tmp[:, :], m)
                        return m
                    linear(layer["q"], h, queries)
                fence()
                dist = sb("distance", [P, T], on=ph2)
                lam = sb("lambda", [P, 4 * HEAD + 8], on=ph2)
                small_ = sb("diff_small", [P, 4, 12], on=ph2)
                subln = sb("subln", [P, 1], on=ph2)
                S = sb("diff_scores", [P, 4, 2, T], on=ph2)
                aT = sb("diff_probs_turned", [P, 4, T], on=ph2)
                O = sb("diff_out", [P, 4, TB, P], on=ph2)
                opnd = Operand("diff_heads", KC, ph2)
                m_dist = load(dist[:, :], K["dist"], c_mask)
                m_lam = load(lam[0:1, 0:4 * HEAD], K["flat_diff_lambda"], c_lam)
                b = take_bank()
                mk = mm(ps[:, b, 0:256], ones[0:1, :], lam[0:1, 0:256], [m_lam, bank_free[b]])
                mk = bank_free[b] = copy(lam[:, 0:256], ps[:, b, 0:256], mk)
                for j in range(2):
                    o = lam[:, 128 * j:128 * j + 64]
                    mk = tt(o, o, lam[:, 128 * j + 64:128 * j + 128], ALU.mult, mk)
                    mk = dve.op(nc.vector.tensor_reduce, mk, lam[:, 256 + j:257 + j], o, AX_X, ALU.add)
                mk = activation(lam[:, 258:260], lam[:, 256:258], ACT.Exp, mk)
                mk = tt(lam[:, 260:261], lam[:, 259:260], lam[:, 258:259], ALU.subtract, mk)
                m_nlam = ts(lam[:, 261:262], lam[:, 260:261], -LAM_INIT, None, ALU.add, None, mk)
                m_subln = ts(subln[:, :], vec("diff_subln"), 1.0 - LAM_INIT, None, ALU.mult, None, None)

                def diff_head(h):
                    def steps(lane):
                        A, B = 2 * lane, 2 * lane + 1
                        s0 = 8.0 * 2.0 ** (-(h + 1))
                        sm = small_[:, lane]
                        o_marks = []
                        for tb in range(TB):
                            n = (tb + 1) * P
                            e_marks = []
                            for c, b in ((0, A), (1, B)):
                                r0 = c * HEAD
                                mk = mm(ps[:, b, 0:n], q[r0:r0 + HEAD, h, tb * P:(tb + 1) * P],
                                        kT[r0:r0 + HEAD, h, 0:n], [bank_free[b]])
                                bank_free[b] = stt(S[:, lane, c, 0:n], dist[:, (TB - 1 - tb) * P:T], s0,
                                                   ps[:, b, 0:n], ALU.mult, ALU.add, [mk, m_dist, lane_free[lane]])
                            yield
                            for c, b in ((0, A), (1, B)):
                                m = dve.op(nc.vector.tensor_reduce, bank_free[b], sm[:, c:c + 1],
                                           S[:, lane, c, 0:n], AX_X, ALU.max)
                                m = ts(sm[:, 2 + c:3 + c], sm[:, c:c + 1], -0.125, None, ALU.mult, None, m)
                                e_marks.append(activation(S[:, lane, c, 0:n], S[:, lane, c, 0:n], ACT.Exp, m,
                                                          bias=sm[:, 2 + c:3 + c], scale=0.125,
                                                          accum_out=sm[:, 4 + c:5 + c]))
                            yield
                            m = dve.op(nc.vector.reciprocal, e_marks, sm[:, 6:8], sm[:, 4:6])
                            m1 = tt(sm[:, 8:9], sm[:, 7:8], lam[:, 261:262], ALU.mult, [m, m_nlam])
                            m = ts(S[:, lane, 0, 0:n], S[:, lane, 0, 0:n], sm[:, 6:7], None, ALU.mult, None, m)
                            m = stt(S[:, lane, 0, 0:n], S[:, lane, 1, 0:n], sm[:, 8:9], S[:, lane, 0, 0:n],
                                    ALU.mult, ALU.add, [m, m1])
                            yield
                            for kt_ in range(tb + 1):
                                mk = turn(ps[:, A, kt_ * P:(kt_ + 1) * P], S[:, lane, 0, kt_ * P:(kt_ + 1) * P],
                                          [m, bank_free[A]])
                            lane_free[lane] = mk
                            m = bank_free[A] = copy(aT[:, lane, 0:n], ps[:, A, 0:n], mk, q=act)
                            yield
                            for kt_ in range(tb + 1):
                                mk = mm(ps[:, B, 0:P], aT[:, lane, kt_ * P:(kt_ + 1) * P],
                                        V[:, kt_, h * P:(h + 1) * P], [m, bank_free[B]],
                                        start=kt_ == 0, stop=kt_ == tb)
                            m = bank_free[B] = copy(O[:, lane, tb], ps[:, B, 0:P], [mk, o_free[lane]], q=act)
                            o_marks.append(m)
                            yield
                        for tb in range(TB):
                            m = activation(aT[:, lane, tb * P:(tb + 1) * P], O[:, lane, tb], ACT.Square, o_marks,
                                           accum_out=small_[:, lane, tb:tb + 1])
                        m = inv_sqrt(small_[:, lane, 4:8], small_[:, lane, 0:4], 1.0 / P, EPS_SUBLN, m)
                        yield
                        for tb in range(TB):
                            m2 = ts(O[:, lane, tb], O[:, lane, tb], small_[:, lane, 4 + tb:5 + tb], None,
                                    ALU.mult, None, m)
                        for tb in range(TB):
                            mk = turn(ps[:, A, tb * P:(tb + 1) * P], O[:, lane, tb], [m2, bank_free[A]])
                        o_free[lane] = mk
                        yield
                        bank_free[A] = opnd.put(h, ps[:, A], [mk, m_subln], subln[:, :])
                    return steps
                lane_free, o_free = [None] * 4, [None] * 4
                interleave([diff_head(h) for h in range(DIFF_HEADS)], 4)
                linear(layer["diff_o"], opnd, add_x)
        fence()

        ffn(layer["ffn11"], "ffn11", 3 * KC)

        with ExitStack() as ph:
            mod = sb("modulation", [P, 24, 2], on=ph)
            gain = sb("mod_gain", [P, KC, 2], on=ph)
            hc = Operand("hc", KC, ph, width=CTX)
            h = Operand("h2", KC, ph)
            with ExitStack() as ph2:
                sc = sb("silu_c", [P, KC, 2], on=ph2)
                row = sb("mod_rows", [2, 3 * C], on=ph2)
                c_in = sb("ctx_in", [P, CTX // P, C], on=ph2)
                cT = sb("ctx_turned", [P, KC, CTX], on=ph2)
                crstd = sb("ctx_rstd", [P, CTX], on=ph2)
                tmp = sb("mod_tmp", [P, 2, T], on=ph2)
                m_ctx = load(c_in[:, :, :], I["ctx_2"][0].rearrange("(b p) c -> p b c", p=P), c_ctx)
                for j, n in enumerate(("c_2", "c_ctx_2")):
                    m_sc = activation(sc[:, :, j], vecs[:, column[n]:column[n] + KC], ACT.Silu, None)
                for bi, ids in enumerate(layer["mod"]):
                    b = take_bank()
                    for uid in ids:
                        u = W.fetch(uid)
                        for kk in range(u["nk"]):
                            k = u["k0"] + kk
                            mk = mm(ps[0:2, b], sc[:, k], u["raw"][:, kk, :],
                                    [m_sc, u["ready"], bank_free[b] if k == 0 else None],
                                    start=k == 0, stop=k == KC - 1)
                        W.done(u, mk)
                    m_row = bank_free[b] = copy(row[:, bi * T:(bi + 1) * T], ps[0:2, b], mk, q=act)
                b = take_bank()
                for i in range(24):
                    mk = turn(ps[:, b, 2 * i:2 * i + 2], row[0:2, i * P:(i + 1) * P], [m_row, bank_free[b]])
                nb = column["b_mod_2"]
                m_mod = bank_free[b] = tt(mod[:, :, :], ps[:, b, 0:48].rearrange("p (i j) -> p i j", j=2),
                                          vecs[:, nb:nb + 24].unsqueeze(2).broadcast_to([P, 24, 2]), ALU.add, mk)
                ng = column["norm_g_2"]
                m_gain = stt(gain[:, :, :], mod[:, KC:2 * KC, :], 1.0,
                             vecs[:, ng:ng + KC].unsqueeze(2).broadcast_to([P, KC, 2]), ALU.add, ALU.mult, m_mod)
                ct_marks = []
                for k in range(KC):
                    b = take_bank()
                    for tb in range(CTX // P):
                        mk = turn(ps[:, b, tb * P:(tb + 1) * P], c_in[:, tb, k * P:(k + 1) * P], [m_ctx, bank_free[b]])
                    bank_free[b] = copy(cT[:, k], ps[:, b, 0:CTX], mk)
                    ct_marks.append(bank_free[b])
                m_crstd = rms([(cT[:, k], ct_marks[k]) for k in range(KC)], dst=crstd[:, :])
                rms_x()
                used = [None, None]
                for j, (src, marks, rs, m_rs, opnd) in enumerate((
                        (x, x_marks, rstd, state["rstd"], h), (cT, ct_marks, crstd, m_crstd, hc))):
                    w = src.shape[2]
                    for k in range(KC):
                        o = tmp[:, k % 2, 0:w]
                        m = tt(o, src[:, k], rs[:, 0:w], ALU.mult, [marks[k], m_rs, used[k % 2]])
                        m = ts(o, o, gain[:, k, j:j + 1], mod[:, k, j:j + 1], ALU.mult, ALU.add, [m, m_gain])
                        used[k % 2] = opnd.put(k, o, m)
            fence()

            o_mla = sb("mla_out", [P, TB, T], on=ph)
            attn_small = sb("attn_small", [P, 4, 4], on=ph)
            LANES = 3

            def attention(name, head_scores, value, o_all, scale, on):
                probs = sb(f"{name}_probs", [P, LANES, KEYS], on=on)
                turned = sb(f"{name}_probs_turned", [P, LANES, KEYS], on=on)
                probs_used = [None] * LANES

                def head(hd):
                    def steps(lane):
                        A, B = 2 * lane, 2 * lane + 1
                        flat = ps[:, A:B + 1].rearrange("p a b -> p (a b)")
                        sm, pr, tu = attn_small[:, lane], probs[:, lane], turned[:, lane]
                        for tb in range(TB):
                            m = head_scores(hd, tb, A, B, [bank_free[A], bank_free[B]], lane)
                            yield
                            m = dve.op(nc.vector.tensor_reduce, m, sm[:, 0:1], flat[:, 0:KEYS], AX_X, ALU.max)
                            m = ts(sm[:, 1:2], sm[:, 0:1], -scale, None, ALU.mult, None, m)
                            m = activation(pr, flat[:, 0:KEYS], ACT.Exp, [m, probs_used[lane]],
                                           bias=sm[:, 1:2], scale=scale, accum_out=sm[:, 2:3])
                            yield
                            m_rs = dve.op(nc.vector.reciprocal, m, sm[:, 3:4], sm[:, 2:3])
                            for kt_ in range(KEYS // P):
                                mk = turn(flat[:, kt_ * P:(kt_ + 1) * P], pr[:, kt_ * P:(kt_ + 1) * P], m)
                            probs_used[lane] = mk
                            yield
                            m = copy(tu, flat[:, 0:KEYS], mk, q=act if tb % 2 else dve)
                            yield
                            for kt_ in range(KEYS // P):
                                mk = mm(ps[:, A, 0:MLA_V], tu[:, kt_ * P:(kt_ + 1) * P], value(hd, kt_), m,
                                        start=kt_ == 0, stop=kt_ == KEYS // P - 1)
                            bank_free[A] = bank_free[B] = ts(o_all[:, tb, hd * MLA_V:(hd + 1) * MLA_V],
                                                             ps[:, A, 0:MLA_V], sm[:, 3:4], None, ALU.mult,
                                                             None, [mk, m_rs])
                            yield
                    return steps
                return head

            with ExitStack() as ph2:
                ka = sb("mla_keys", [QK, MLA_HEADS, KEYS], on=ph2)
                qa = sb("mla_queries", [QK, MLA_HEADS, T], on=ph2)
                va = sb("mla_values", [P, KEYS // P, MLA_HEADS * MLA_V], on=ph2)
                with ExitStack() as ph3:
                    cosm = sb("cosines", [QK, T], on=ph3)
                    sinm = sb("sines", [QK, T], on=ph3)
                    swap = sb("swap", [QK, QK], on=ph3)
                    ckv = Operand("ckv", 1, ph3)
                    cckv = Operand("cckv", 1, ph3, width=CTX)
                    small = sb("mla_tmp", [P, 2, T], on=ph3)
                    with ExitStack() as ph4:
                        for dst, n in ((cosm, "cos"), (sinm, "sin"), (swap, "swap")):
                            m_rope = load(dst[:, :], K[n], c_mask)
                        for q_ in (dve, pe):
                            q_.wait(m_rope)
                        fence_tmp = [None, None]
                        def latent(opnd, width, k_at, rotate):
                            def evac(bi, i, b, mark):
                                if i == 0:
                                    m = copy(small[:, 0, 0:width], ps[:, b, 0:width], [mark, fence_tmp[0]])
                                    r = rms([(small[:, 0, 0:width], m)], dst=small[:, 1, 0:width], channels=P)
                                    n = tt(small[:, 0, 0:width], small[:, 0, 0:width], small[:, 1, 0:width], ALU.mult, r)
                                    fence_tmp[0] = opnd.put(0, small[:, 0, 0:width], n, vec("g_ckv_2"))
                                    return m
                                rows = slice(NOPE, QK)
                                dst = ka[rows, 0, k_at:k_at + width]
                                m0 = m = copy(dst, ps[rows, b, 0:width], mark)
                                if rotate:
                                    b2 = take_bank()
                                    mk = mm(ps[0:QK, b2, 0:width], swap[rows, :], dst, [m, bank_free[b2]])
                                    s = small[rows, 1, 0:width]
                                    m2 = bank_free[b2] = tt(s, ps[rows, b2, 0:width], sinm[rows, 0:width], ALU.mult,
                                                            [mk, fence_tmp[0]])
                                    m = tt(dst, dst, cosm[rows, 0:width], ALU.mult, mk)
                                    fence_tmp[0] = m = tt(dst, dst, s, ALU.add, [m, m2])
                                for j in range(1, MLA_HEADS):
                                    copy(ka[rows, j, k_at:k_at + width], dst, m, q=pool)
                                return m0
                            return evac
                        linear(layer["ckv"], h, latent(ckv, T, 0, True), tiles=[(0, P), (NOPE, QK)],
                               extra=(hc, latent(cckv, CTX, T, False)))

                        def key_part(k_at, width):
                            def evac(bi, i, b, mark):
                                return copy(ka[0:NOPE, 4 * bi + i, k_at:k_at + width], ps[0:NOPE, b, 0:width],
                                            mark, q=act)
                            return evac
                        linear(layer["uk"], ckv, key_part(0, T), extra=(cckv, key_part(T, CTX)))

                        def value_part(t0):
                            def evac(bi, i, b, mark):
                                return copy(va[:, t0 + i], ps[:, b], mark, q=act)
                            return evac
                        linear(layer["uv"], ckv, value_part(0), natural=True, extra=(cckv, value_part(TB)))
                    with ExitStack() as ph4:
                        cq = Operand("cq", 2, ph4)
                        raw_q = o_mla[:, 0:2]
                        raw_marks = [None, None]

                        def cq_part(bi, i, b, mark):
                            raw_marks[i] = copy(raw_q[:, i], ps[:, b], mark, q=act)
                            return raw_marks[i]
                        linear(layer["cq"], h, cq_part)
                        r = rms([(raw_q[:, i], raw_marks[i]) for i in range(2)], dst=small[:, 1],
                                channels=2 * P, after=[dve.now(), pool.now()])
                        for i in range(2):
                            m = tt(raw_q[:, i], raw_q[:, i], small[:, 1], ALU.mult, r)
                            cq.put(i, raw_q[:, i], m, vec("g_cq_2", i))

                        def q_part(bi, i, b, mark):
                            hd = 4 * bi + i
                            m0 = m = copy(qa[:, hd], ps[0:QK, b], mark, q=act)
                            b2 = take_bank()
                            mk = mm(ps[0:QK, b2], swap[:, :], qa[:, hd], [m, bank_free[b2]])
                            s = small[0:QK, hd % 2]
                            m2 = bank_free[b2] = tt(s, ps[0:QK, b2], sinm[:, :], ALU.mult, [mk, m])
                            m = tt(qa[:, hd], qa[:, hd], cosm[:, :], ALU.mult, [mk])
                            tt(qa[:, hd], qa[:, hd], s, ALU.add, [m, m2])
                            return m0
                        linear(layer["uq"], cq, q_part, tiles=[(i * QK, QK) for i in range(4)])
                fence()

                def mla_scores(hd, tb, A, B, free, lane):
                    l = qa[:, hd, tb * P:(tb + 1) * P]
                    mm(ps[:, A], l, ka[:, hd, 0:T], free)
                    return mm(ps[:, B, 0:CTX], l, ka[:, hd, T:KEYS], None)
                head = attention("mla", mla_scores, lambda hd, kt_: va[:, kt_, hd * MLA_V:(hd + 1) * MLA_V],
                                 o_mla, QK ** -0.5, ph2)
                interleave([head(hd) for hd in range(MLA_HEADS)], LANES)
            fence()

            o_na = sb("na_out", [P, TB, T], on=ph)
            with ExitStack() as ph2:
                kb = sb("na_keys", [P, 4, KEYS], on=ph2)
                qb = sb("na_queries", [P, 4, T], on=ph2)
                vb = sb("na_values", [P, KEYS // P, T], on=ph2)
                bias = sb("window_bias", [P, LANES, NA_OFF, GRID_W], on=ph2)
                wmask = sb("window_mask", [P, GRID_W], on=ph2)
                m_wmask = load(wmask[:, :], K["window"], c_mask)

                def turned_keys(k_at, width):
                    return lambda bi, i, b, mark: copy(kb[:, i, k_at:k_at + width], ps[:, b, 0:width], mark, q=act)
                linear(layer["kb"], h, turned_keys(0, T), extra=(hc, turned_keys(T, CTX)))

                def natural_values(t0):
                    return lambda bi, i, b, mark: copy(vb[:, t0 + i], ps[:, b], mark, q=act)
                linear(layer["vb"], h, natural_values(0), natural=True, extra=(hc, natural_values(TB)))

                linear(layer["qb"], h, lambda bi, i, b, mark: activation(
                    qb[:, i], ps[:, b], ACT.Copy, mark, scale=0.125))
                ready = [act.now()]
                bias_marks, bias_used = [None] * NA_HEADS, [None] * NA_HEADS

                def load_bias(hd):
                    s = hd % LANES
                    for parity in range(2):
                        src = I["rpb_2"][hd, :, 1 - parity:1 - parity + NA_OFF, :]
                        m = load(bias[parity * GRID_W:(parity + 1) * GRID_W, s], src, c_bias[s],
                                 bias_used[hd - LANES] if hd >= LANES else None)
                    wm = wmask[:, :].unsqueeze(1).broadcast_to([P, NA_OFF, GRID_W])
                    bias_marks[hd] = tt(bias[:, s], bias[:, s], wm, ALU.add,
                                        [m, m_wmask], q=pool)

                def na_scores(hd, tb, A, B, free, lane):
                    if tb == 0 and bias_marks[hd] is None:
                        load_bias(hd)
                    h0, kt_ = (hd % 2) * HEAD, hd // 2
                    l = qb[h0:h0 + HEAD, kt_, tb * P:(tb + 1) * P]
                    mk = mm(ps[:, A], l, kb[h0:h0 + HEAD, kt_, 0:T], [free, ready])
                    mk2 = mm(ps[:, B, 0:CTX], l, kb[h0:h0 + HEAD, kt_, T:KEYS], None)
                    e0 = NA_KR - 2 - 2 * tb
                    v = bias[:, hd % LANES, e0:e0 + NA_KR, :].rearrange("p e c -> p (e c)")
                    m = tt(ps[:, A], ps[:, A], v, ALU.add, [mk2, bias_marks[hd]])
                    bias_used[hd] = m
                    return m
                head = attention("na", na_scores, lambda hd, kt_: vb[:, kt_, hd * MLA_V:(hd + 1) * MLA_V],
                                 o_na, 1.0, ph2)
                interleave([head(hd) for hd in range(NA_HEADS)], LANES)
            fence()

            with ExitStack() as ph2:
                z = sb("silu_z", [P, 4, T], on=ph2)
                g = sb("sigmoid_g", [P, KC, T], on=ph2)
                y = sb("y", [P, KC, T], on=ph2)
                gated = Operand("gated", 4, ph2)
                gtmp = sb("gated_tmp", [P, 2, T], on=ph2)
                g_marks, y_marks = [None] * KC, [None] * KC
                g_used, z_used, gt_used = [None] * KC, [None] * 4, [None, None]
                for branch, (zn, gn, wn, o_all) in enumerate((("za", "ga", "w_oa", o_mla), ("zb", "gb", "w_ob", o_na))):
                    def silu_z(bi, i, b, mark):
                        z_marks[i] = activation(z[:, i], ps[:, b], ACT.Silu, [mark, z_used[i]])
                        return z_marks[i]

                    def sigmoid_g(bi, i, b, mark):
                        k = 4 * bi + i
                        g_marks[k] = activation(g[:, k], ps[:, b], ACT.Sigmoid, [mark, g_used[k]])
                        return g_marks[k]

                    def gate_y(bi, i, b, mark, branch=branch):
                        k = 4 * bi + i
                        if branch == 0:
                            g_used[k] = y_marks[k] = tt(y[:, k], ps[:, b], g[:, k], ALU.mult, [mark, g_marks[k]])
                            return y_marks[k]
                        m = tt(g[:, k], ps[:, b], g[:, k], ALU.mult, [mark, g_marks[k]])
                        y_marks[k] = tt(y[:, k], y[:, k], g[:, k], ALU.add, [m, y_marks[k]])
                        return m
                    z_marks = [None] * 4
                    linear(layer[zn], h, silu_z)
                    for k in range(4):
                        b = take_bank()
                        for tb in range(TB):
                            mk = turn(ps[:, b, tb * P:(tb + 1) * P], o_all[:, tb, k * P:(k + 1) * P], bank_free[b])
                        m = bank_free[b] = tt(gtmp[:, k % 2], ps[:, b], z[:, k], ALU.mult,
                                              [mk, z_marks[k], gt_used[k % 2]])
                        z_used[k] = m
                        gt_used[k % 2] = gated.put(k, gtmp[:, k % 2], m)
                    linear(layer[gn], h, sigmoid_g)
                    h.used = pe.now()
                    linear(layer[wn], gated, gate_y)
                    gated.used = pe.now()
                for k in range(KC):
                    h.put(k, y[:, k], y_marks[k])

                def add_gated(bi, i, b, mark):
                    k = 4 * bi + i
                    x_marks[k] = stt(x[:, k], ps[:, b], mod[:, 2 * KC + k, 0:1], x[:, k], ALU.mult, ALU.add,
                                     [mark, x_marks[k], act.now()])
                    return x_marks[k]
                linear(layer["w_out"], h, add_gated)
        fence()

        with ExitStack() as ph:
            y = sb("normed", [P, KC, T], on=ph)
            o = sb("out_rows", [P, TB, C], on=ph)
            rms_x()
            for k in range(KC):
                m = stt(y[:, k], x[:, k], vec("final_g_2", k), rstd[:, :], ALU.mult, ALU.mult, state["rstd"])
                b = take_bank()
                for tb in range(TB):
                    mk = turn(ps[:, b, tb * P:(tb + 1) * P], y[:, k, tb * P:(tb + 1) * P], [m, bank_free[b]])
                m = bank_free[b] = copy(o[:, :, k * P:(k + 1) * P], ps[:, b].rearrange("p (b c) -> p b c", c=P), mk,
                                        q=act if k % 2 else dve)
            m_out = load(out[0].rearrange("(b p) c -> p b c", p=P), o[:, :, :], c_out, act.now(), dve.now())
            sp.wait(m_out)

        with nc.Block() as block:
            @block.sync
            def _(engine):
                sp.emit(engine)

            @block.scalar
            def _(engine):
                act.emit(engine)

            @block.vector
            def _(engine):
                dve.emit(engine)

            @block.gpsimd
            def _(engine):
                pool.emit(engine)

            @block.tensor
            def _(engine):
                pe.emit(engine)


def tables():
    i, j = np.arange(P)[:, None], np.arange(P)[None, :]
    same = i // CHUNK == j // CHUNK
    f = lambda a: np.ascontiguousarray(a, dtype=np.float32)
    heads = f(i // HEAD == j // HEAD)
    t = {"ident": f(i == j), "headsum": heads, "center": f(i == j) - heads / HEAD}
    t["masks"] = f(np.concatenate([same & (i < j), same & (i <= j)], 1))
    near = (i // 2 == j // 2)
    t["seed"] = f(np.concatenate([near & (i > j), near & (i < j)], 1))
    t["level"] = f(np.concatenate([(i // (2 * s) == j // (2 * s)) & (i % (2 * s) >= s) & (j % (2 * s) < s)
                                   for s in (2, 4, 8, 16, 32)], 1))
    t["run"] = f(np.broadcast_to(np.arange(T) % CHUNK != 0, (P, T)))
    d = np.arange(T)[None, :] - (T - P) - i
    t["dist"] = f(np.where(d > 0, NEG, d))
    half = ROPE // 4
    freqs = np.float32(10000.0) ** (-np.arange(half, dtype=np.float32) / np.float32(half))
    cos, sin = np.ones((QK, T), np.float32), np.zeros((QK, T), np.float32)
    swap = np.zeros((QK, QK), np.float32)
    tok = np.arange(T)
    for part, pos in enumerate((tok // GRID_W, tok % GRID_W)):
        ang = pos.astype(np.float32)[None, :] * freqs[:, None].astype(np.float32)
        base = NOPE + part * 2 * half
        for s in range(2):
            rows = slice(base + s * half, base + (s + 1) * half)
            cos[rows], sin[rows] = np.cos(ang), np.sin(ang)
        for c in range(half):
            swap[base + half + c, base + c] = -1.0
            swap[base + c, base + half + c] = 1.0
    t.update(cos=cos, sin=sin, swap=swap)
    col, start = np.arange(GRID_W), np.clip(np.arange(GRID_W) - NA_KC // 2, 0, GRID_W - NA_KC)
    inside = (col[None, :] >= start[:, None]) & (col[None, :] < start[:, None] + NA_KC)
    t["window"] = f(np.tile(np.where(inside, 0.0, NEG), (2, 1)))
    return t


_INS = ['x', 'ffn_norm', 'ffn_w_in', 'ffn_w_out', 'mix_norm', 'rwkv_mu', 'rwkv_w_rkv', 'rwkv_w0', 'rwkv_w1',
        'rwkv_w2', 'rwkv_a0', 'rwkv_a1', 'rwkv_a2', 'rwkv_g1', 'rwkv_g2', 'rwkv_k_k', 'rwkv_k_a', 'rwkv_r_k',
        'rwkv_ln_g', 'rwkv_ln_b', 'rwkv_w_o', 'kv_norm', 'w_kv', 'k_norm', 'diff_w_q', 'diff_q_norm',
        'diff_lambda', 'diff_subln', 'diff_w_o', 'c_2', 'ctx_2', 'c_ctx_2', 'w_mod_2', 'b_mod_2', 'norm_g_2',
        'w_in_2', 'g_cq_2', 'w_uq_2', 'g_ckv_2', 'w_ukv_2', 'rpb_2', 'w_oa_2', 'w_ob_2', 'w_out_2', 'final_g_2']
PAD = GRID_W - NA_KC


def kernel(**inputs):
    import concourse.bacc as _bacc
    from concourse.bass_utils import run_bass_kernel_spmd as _run

    nc = _bacc.Bacc("TRN2", target_bir_lowering=False, num_devices=1)
    arrays, aps = {}, {}

    def give(name, a):
        arrays[f"in_{name}_dram"] = np.ascontiguousarray(a)
        return nc.dram_tensor(f"in_{name}_dram", a.shape, mybir.dt.from_np(a.dtype), kind="ExternalInput").ap()

    for name in _INS:
        a = np.asarray(inputs[name])
        if name == "rpb_2":
            a = np.pad(a[0], ((0, 0), (0, 0), (PAD, PAD)))
            a = np.stack([a[:, :, GRID_W - 1 - w:2 * GRID_W - 1 - w] for w in range(GRID_W)], axis=1)
        aps[name] = give(name, a)
    consts = {n: give("table_" + n, a) for n, a in tables().items()}
    for name, n in PACK1 + PACK2 + [("diff_lambda", 1)]:
        ap = aps[name]
        while len(ap.shape) > 1:
            ap = ap.rearrange("a b -> (a b)" if len(ap.shape) == 2 else
                              "a b c -> (a b) c" if len(ap.shape) == 3 else "a b c d -> (a b) c d")
        size = ap.shape[0]
        rows = 1 if size < P or name == "diff_lambda" else n
        consts["flat_" + name] = ap.rearrange("(r c) -> r c", r=rows)
    out = nc.dram_tensor("out_0_dram", (1, T, C), F32, kind="ExternalOutput").ap()
    program(nc, aps, consts, out)
    r = _run(nc, [arrays], core_ids=[0])
    return r.results[0]["out_0_dram"]
```

```python
import math
from contextlib import ExitStack

import numpy as np

import concourse.bass as bass
from concourse import mybir

F32 = mybir.dt.float32
F32R = mybir.dt.float32r
ALU = mybir.AluOpType
ACT = mybir.ActivationFunctionType
AX_X = mybir.AxisListType.X

P = 128
C = 1024
KC = C // P
T = 512
TB = T // P
F = 2816
KF = F // P
CTX = 256
HEAD = 64
CHUNK = 64
NCH = T // CHUNK
DIFF_HEADS = 8
MLA_HEADS, NOPE, ROPE, MLA_V = 8, 64, 32, 64
QK = NOPE + ROPE
NA_HEADS, NA_KC, GRID_W, NA_KR = 8, 16, 64, 8
NA_OFF = 2 * NA_KR - 2
KEYS = T + CTX
WKV_SKEW = 13
NEG = -1.0e30

PACK1 = [("ffn_norm", 32), ("mix_norm", 16), ("rwkv_mu", 48)]
PACK2 = [("rwkv_w0", 8), ("rwkv_a0", 8), ("rwkv_k_k", 8), ("rwkv_k_a", 8), ("rwkv_r_k", 8),
         ("rwkv_ln_g", 8), ("rwkv_ln_b", 8), ("kv_norm", 8), ("norm_g_2", 8), ("final_g_2", 8),
         ("b_mod_2", 24), ("diff_subln", 1), ("g_cq_2", 2), ("g_ckv_2", 1), ("c_2", 8),
         ("c_ctx_2", 8), ("diff_q_norm", 1), ("k_norm", 1)]


class Queue:

    def __init__(self, sem):
        self.sem, self.count, self.items, self.waited = sem, 0, [], {}

    def wait(self, *marks):
        for m in marks:
            if m is None:
                continue
            if isinstance(m, list):
                self.wait(*m)
                continue
            sem, value = m
            if self.waited.get(id(sem), 0) < value:
                self.waited[id(sem)] = value
                self.items.append((None, (sem, value), {}, None))

    def op(self, issue, after, *args, **kw):
        self.wait(after)
        self.count += 1
        self.items.append((issue, args, kw, (self.sem, 1)))
        return (self.sem, self.count)

    def quiet(self, issue, after, *args, **kw):
        self.wait(after)
        self.items.append((issue, args, kw, None))

    def dma(self, issue, out, in_, counter, *after):
        self.wait(*after)
        counter[1] += 16
        self.items.append((issue, (out, in_), {}, (counter[0], 16)))
        return (counter[0], counter[1])

    def now(self):
        return (self.sem, self.count) if self.count else None

    def emit(self, engine):
        for issue, args, kw, inc in self.items:
            if issue is None:
                engine.wait_ge(*args)
                continue
            made = issue(*args, **kw)
            if inc:
                made.then_inc(*inc)


class Weights:

    RAW, CONV, AHEAD = 4, 3, 2

    def __init__(self, nc, raw, hi, lo, counters, sp, act, dve):
        self.nc, self.raw, self.hi, self.lo, self.counters = nc, raw, hi, lo, counters
        self.sp, self.act, self.dve = sp, act, dve
        self.units, self.prepared, self.nconv = [], 0, 0
        self.raw_free = [None] * self.RAW
        self.conv_free = [None] * self.CONV

    def plan(self, rows, blocks, direct=False, nk=2, base=0):
        out = []
        for cols in blocks:
            ids, k = [], 0
            while k * P < rows:
                n = min(nk, (rows - k * P) // P) or 1
                part = min(P, rows - k * P)
                self.units.append(dict(k0=k, nk=n, part=part, cols=cols, direct=direct, base=base))
                ids.append(len(self.units) - 1)
                k += n
            out.append(ids)
        return out

    def _prepare(self, i):
        u = self.units[i]
        slot, n, p, at, p0 = i % self.RAW, u["nk"], u["part"], 0, u["base"]
        for view in u["cols"]:
            src = view(u["k0"] * P, n * p, p)
            width = int(np.prod(src.shape[2:]))
            dst = self.raw[p0:p0 + p, slot, 0:n, at:at + width]
            if n == 1:
                dst, src = dst[:, 0], src[:, 0]
            if len(src.shape) == 3 and n == 1:
                dst = dst.rearrange("p (a b) -> p a b", b=src.shape[2])
            arrived = self.sp.dma(self.nc.sync.dma_start, dst, src, self.counters[slot], self.raw_free[slot])
            at += width
        u["width"], u["raw"] = at, self.raw[:, slot]
        if u["direct"]:
            u["ready"], u["slot"] = arrived, slot
            return
        c = self.nconv % self.CONV
        self.nconv += 1
        src = self.raw[0:p, slot, 0:n, 0:at]
        hi, lo = self.hi[0:p, c, 0:n, 0:at], self.lo[0:p, c, 0:n, 0:at]
        a = self.act.op(self.nc.scalar.activation, [arrived, self.conv_free[c]], hi, src, ACT.Copy)
        v = self.dve.op(self.nc.vector.tensor_tensor, a, lo, src, hi.bitcast(F32), ALU.subtract)
        self.raw_free[slot] = [a, v]
        u["ready"], u["slot"], u["hi"], u["lo"] = v, c, self.hi[:, c], self.lo[:, c]

    def fetch(self, i):
        while self.prepared < min(len(self.units), i + 1 + self.AHEAD):
            self._prepare(self.prepared)
            self.prepared += 1
        return self.units[i]

    def done(self, u, mark):
        if u["direct"]:
            self.raw_free[u["slot"]] = mark
        else:
            self.conv_free[u["slot"]] = mark


def interleave(lanes, width):
    lanes, live, free = list(lanes), [], list(range(width))
    while lanes or live:
        while lanes and free:
            lane = free.pop(0)
            live.append((lanes.pop(0)(lane), lane))
        for g, lane in list(live):
            try:
                next(g)
            except StopIteration:
                live.remove((g, lane))
                free.append(lane)


def program(nc, I, K, out):
    with ExitStack() as ctx:
        def sb(name, shape, dt=F32, on=None):
            return (on or ctx).enter_context(nc.sbuf_tensor(name, shape, dt))

        def dma_counter(name):
            return [ctx.enter_context(nc.semaphore(name)), 0]

        act, dve, pool, pe, sp = (Queue(ctx.enter_context(nc.semaphore(f"{n}_done")))
                                  for n in ("act", "dve", "pool", "pe", "sp"))
        c_const, c_pack, c_x, c_ctx, c_out, c_lam, c_mask, c_spill = (dma_counter(n) for n in (
            "consts_in", "packs_in", "x_in", "ctx_in", "out_stored", "lambda_in", "masks_in", "x_spilled"))
        c_ring = [dma_counter(f"weights_in{i}") for i in range(Weights.RAW)]
        c_bias = [dma_counter(f"bias_in{i}") for i in range(3)]

        def activation(dst, src, func, after, **kw):
            return act.op(nc.scalar.activation, after, dst, src, func, **kw)

        def tt(dst, a, b, op, after, q=None):
            q = q or dve
            f = nc.gpsimd.tensor_tensor if q is pool else nc.vector.tensor_tensor
            return q.op(f, after, dst, a, b, op)

        def stt(dst, a, scalar, b, op0, op1, after):
            return dve.op(nc.vector.scalar_tensor_tensor, after, out=dst, in0=a, scalar=scalar,
                          in1=b, op0=op0, op1=op1)

        def ts(dst, a, s1, s2, op0, op1, after):
            if s2 is None:
                return dve.op(nc.vector.tensor_scalar, after, dst, a, s1, None, op0)
            return dve.op(nc.vector.tensor_scalar, after, dst, a, s1, s2, op0, op1)

        def copy(dst, src, after, q=None):
            q = q or dve
            if q is act:
                return activation(dst, src, ACT.Copy, after)
            return q.op(nc.gpsimd.tensor_copy if q is pool else nc.vector.tensor_copy, after, dst, src)

        def mm(dst, lhsT, rhs, after, start=True, stop=True, mark=True, **kw):
            return (pe.op if mark else pe.quiet)(nc.tensor.matmul, after, dst, lhsT, rhs,
                                                 start=start, stop=stop, **kw)

        def turn(dst, src, after, mark=True):
            n = src.shape[0]
            return (pe.op if mark else pe.quiet)(nc.tensor.transpose, after, dst, src, ident[0:n, 0:n])

        def load(dst, src, counter, *after):
            return sp.dma(nc.sync.dma_start, dst, src, counter, *after)

        ps = ctx.enter_context(nc.psum_tensor("banks", [P, 8, T], F32))
        bank_free = [None] * 8
        next_bank = [0]

        held_banks = set()

        def take_bank():
            while True:
                next_bank[0] = (next_bank[0] + 1) % 8
                if next_bank[0] not in held_banks:
                    return next_bank[0]

        later = []

        def after_units(n, fn):
            later.append([n, fn])

        def tick():
            for entry in later:
                entry[0] -= 1
            due = [e for e in later if e[0] <= 0]
            later[:] = [e for e in later if e[0] > 0]
            for _, fn in due:
                fn()

        def flush_later():
            while later:
                tick()

        ring_raw = sb("weights_raw", [P, Weights.RAW, 2, 512])
        ring_hi = sb("weights_hi", [P, Weights.CONV, 2, 512], F32R)
        ring_lo = sb("weights_lo", [P, Weights.CONV, 2, 512], F32R)
        x = sb("x_turned", [P, KC, T])
        ident = sb("ident", [P, P])
        ones = sb("ones", [P, P])
        headsum = sb("headsum", [P, P])
        vecs = sb("vectors", [P, 256])
        rstd = sb("rstd", [P, T])
        sq = sb("squares", [P, 2, T])
        sq_sum = sb("squares_sum", [P, T])
        eps = sb("eps", [P, 4])
        W = Weights(nc, ring_raw, ring_hi, ring_lo, c_ring, sp, act, dve)
        column = {}
        for base, pack in ((0, PACK1), (P, PACK2)):
            for name, n in pack:
                column[name] = base
                base += n

        def vec(name, k=0):
            return vecs[:, column[name] + k:column[name] + k + 1]

        def columns(w, c0, c1):
            return lambda r0, n, part: w[r0:r0 + n, c0:c1].rearrange("(k p) n -> p k n", p=part)

        def dense(w, step=512, c0=0, c1=None, **kw):
            c1 = c1 or w.shape[1]
            return W.plan(w.shape[0], [[columns(w, c, min(c + step, c1))] for c in range(c0, c1, step)], **kw)

        def ffn_plan(l, s):
            w_in, w_out = I["ffn_w_in"][l, s], I["ffn_w_out"][l, s]
            parts = []
            for f0, f1 in ((0, KF // 2 + 1), (KF // 2 + 1, KF)):
                gate_up = W.plan(C, [[columns(w_in, f * P, (f + 2) * P), columns(w_in, F + f * P, F + (f + 2) * P)]
                                     for f in range(f0, f1, 2)])
                parts.append((gate_up, dense(w_out[f0 * P:f1 * P, :])))
            return parts

        w_in2, w_ukv, w_uq = I["w_in_2"][0], I["w_ukv_2"][0], I["w_uq_2"][0]
        span, at = {}, 0
        for n, w in (("ckv", 128), ("kr", 32), ("kb", 512), ("vb", 512), ("cq", 256), ("za", 512),
                     ("qb", 512), ("zb", 512), ("ga", 1024), ("gb", 1024)):
            span[n] = (at, at + w)
            at += w

        def w_in_part(n):
            return dense(w_in2, c0=span[n][0], c1=span[n][1])

        layer = {"ffn00": ffn_plan(0, 0)}
        for n in ("w1", "a1", "g1"):
            layer[n] = dense(I[f"rwkv_{n}"][0], direct=True)
        for s in range(3):
            layer["rkv", s] = dense(I["rwkv_w_rkv"][0, s])
        for m in range(KC):
            for n in ("w2", "a2", "g2"):
                layer[n, m] = dense(I[f"rwkv_{n}"][0], c0=m * P, c1=m * P + P, direct=True, nk=1,
                                    base=64 if n == "a2" else 0)
        layer["rwkv_o"] = dense(I["rwkv_w_o"][0])
        layer["ffn01"] = ffn_plan(0, 1)
        layer["kv"] = dense(I["w_kv"])
        layer["ffn10"] = ffn_plan(1, 0)
        layer["q"] = dense(I["diff_w_q"][0])
        layer["diff_o"] = dense(I["diff_w_o"][0])
        layer["ffn11"] = ffn_plan(1, 1)
        layer["mod"] = dense(I["w_mod_2"][0], direct=True)
        layer["ckv"] = W.plan(C, [[columns(w_in2, 0, 160)]])
        layer["uk"] = dense(w_ukv)
        layer["uv"] = W.plan(P, [[lambda r0, n, part: w_ukv.rearrange(
            "(k p) (h c) -> p k h c", p=part, c=P)[:, :, :, NOPE:P]]])
        layer["cq"] = w_in_part("cq")
        layer["uq"] = dense(w_uq, step=4 * QK)
        for n in ("kb", "vb", "qb", "za", "ga"):
            layer[n] = w_in_part(n)
        layer["w_oa"] = dense(I["w_oa_2"][0])
        layer["zb"] = w_in_part("zb")
        layer["gb"] = w_in_part("gb")
        layer["w_ob"] = dense(I["w_ob_2"][0])
        layer["w_out"] = dense(I["w_out_2"][0])

        def linear(blocks, operand, evac, **kw):
            for _ in linear_steps(blocks, operand, evac, **kw):
                tick()

        def linear_steps(blocks, operand, evac, natural=False, tiles=None, extra=None, freed=None):
            for bi, ids in enumerate(blocks):
                width = W.fetch(ids[0])["width"]
                jobs = []
                for opnd, ev in [(operand, evac)] + ([extra] if extra else []):
                    ntok = opnd(0)[0].shape[1]
                    spans = ([(c, P) for c in range(0, ntok, P)] if natural else
                             tiles or [(c, P) for c in range(0, width, P)])
                    for i, (c0, m) in enumerate(spans):
                        b = take_bank()
                        held_banks.add(b)
                        jobs.append((opnd, ev, i, c0, m, b, ntok))
                for uid in ids:
                    u = W.fetch(uid)
                    for opnd, ev, i, c0, m, b, ntok in jobs:
                        for kk in range(u["nk"]):
                            xh, xl, ready = opnd(u["k0"] + kk)
                            first, last = u["k0"] + kk == 0, uid == ids[-1] and kk == u["nk"] - 1
                            if natural:
                                o = ps[:, b, 0:width]
                                wh, wl = u["hi"][:, kk, 0:width], u["lo"][:, kk, 0:width]
                                xh, xl = xh[:, c0:c0 + m], xl[:, c0:c0 + m]
                                terms = ((xh, wh), (xh, wl), (xl, wh))
                            else:
                                o = ps[0:m, b, 0:ntok]
                                wh, wl = u["hi"][:, kk, c0:c0 + m], u["lo"][:, kk, c0:c0 + m]
                                terms = ((wh, xh), (wh, xl), (wl, xh))
                            for t, (l, r) in enumerate(terms):
                                mark = mm(o, l, r, [u["ready"], ready, bank_free[b] if first else None],
                                          start=first and t == 0, stop=last and t == 2,
                                          mark=t == 2 and kk == u["nk"] - 1)
                        for kk in range(u["nk"]):
                            opnd.used[u["k0"] + kk] = mark
                        if uid == ids[-1]:
                            bank_free[b] = ev(bi, i, b, mark)
                            held_banks.discard(b)
                    W.done(u, mark)
                    if freed and bi == len(blocks) - 1:
                        for kk in range(u["nk"]):
                            freed(u["k0"] + kk)
                    yield

        def split(hi, lo, src, after, scale=None):
            if scale is None:
                h = activation(hi, src, ACT.Copy, after)
                return [h, tt(lo, src, hi.bitcast(F32), ALU.subtract, h)]
            h = activation(hi, src, ACT.Copy, after, scale=scale)
            return [h, stt(lo, src, scale, hi.bitcast(F32), ALU.mult, ALU.subtract, h)]

        class Operand:

            def __init__(self, name, tiles, on, width=T):
                self.hi = sb(f"{name}_hi", [P, tiles, width], F32R, on=on)
                self.lo = sb(f"{name}_lo", [P, tiles, width], F32R, on=on)
                self.marks = [None] * tiles
                self.used = [None] * tiles

            def put(self, k, src, after, scale=None):
                self.marks[k] = split(self.hi[:, k], self.lo[:, k], src, [after, self.used[k]], scale)
                return self.marks[k]

            def __call__(self, k):
                return self.hi[:, k], self.lo[:, k], self.marks[k]

        def fence():
            marks = [q.now() for q in (act, dve, pool, pe)]
            for q in (act, dve, pool, pe, sp):
                q.wait(*marks)

        def inv_sqrt(dst, src, scale, eps_col, after):
            n = dst.shape[0]
            r = activation(dst, src, ACT.Sqrt, after, bias=eps[0:n, eps_col:eps_col + 1], scale=scale)
            return dve.op(nc.vector.reciprocal, r, dst, dst)

        OP = Operand("operand", KC, ctx)

        EPS_NORM, EPS_RWKV, EPS_SUBLN, EPS_NONE = range(4)
        x_marks = [None] * KC
        state = {"sum_used": None, "sum": None, "rstd": None, "rstd_read": None, "tmp_used": None}
        sq_used = [None, None]

        def square(k, tile, mark):
            w = tile.shape[1]
            a = activation(sq[:, k % 2, 0:w], tile, ACT.Square, [mark, sq_used[k % 2]])
            if k == 0:
                m = copy(sq_sum[:, 0:w], sq[:, 0, 0:w], [a, state["sum_used"]])
            else:
                m = tt(sq_sum[:, 0:w], sq_sum[:, 0:w], sq[:, k % 2, 0:w], ALU.add, [a, state["sum"]])
            sq_used[k % 2] = state["sum"] = m
            return a

        def finish_rms(dst, after, channels=C):
            w = dst.shape[1]
            b = take_bank()
            p = mm(ps[:, b, 0:w], ones[:, :], sq_sum[:, 0:w], [state["sum"], consts, bank_free[b]])
            state["sum_used"] = p
            r = inv_sqrt(dst, ps[:, b, 0:w], 1.0 / channels, EPS_NORM, [p, after])
            bank_free[b] = r
            return r

        def rms(tiles, dst, after=None, channels=C):
            for k, (t, m) in enumerate(tiles):
                square(k, t, m)
            return finish_rms(dst, after, channels)

        x_read = [None] * KC

        def finish_x():
            state["rstd"] = finish_rms(rstd[:, :], state["rstd_read"])

        def feed(k, gain=None, k0=0):
            x_read[k] = [square(k, x[:, k], x_marks[k])]
            if gain:
                x_read[k].append(OP.put(k, x[:, k], x_marks[k], vec(gain, k0 + k))[0])

        def times_rstd(dst, b, mark, after=None):
            m = tt(dst, ps[:, b], rstd[:, :], ALU.mult, [mark, state["rstd"], after])
            state["rstd_read"] = m
            return m

        def head_norm(dst, gain, tmp, after):
            a = activation(sq[:, 0, :], dst, ACT.Square, [after, sq_used[0]])
            b = take_bank()
            p = mm(ps[:, b], headsum[:, :], sq[:, 0], [a, bank_free[b]])
            sq_used[0] = p
            r = inv_sqrt(tmp, ps[:, b], 1.0 / HEAD, EPS_NORM, [p, state["tmp_used"]])
            bank_free[b] = r
            state["tmp_used"] = stt(dst, dst, gain, tmp, ALU.mult, ALU.mult, r)
            return state["tmp_used"]

        load(ident[:, :], K["ident"], c_const)
        m_const = load(headsum[:, :], K["headsum"], c_const)
        m = pool.op(nc.gpsimd.memset, None, ones[:, :], 1.0)
        for i, v in enumerate((1e-6, 64e-5, 1e-5, 0.0)):
            m = pool.op(nc.gpsimd.memset, None, eps[:, i:i + 1], v)
        consts = [m_const, m]
        with ExitStack() as ph:
            packs = sb("packs", [P, 2, P], on=ph)
            x_in = sb("x_in", [P, TB, C], on=ph)
            m_x = load(x_in[:, :, :], I["x"][0].rearrange("(b p) c -> p b c", p=P), c_x)
            clear = dve.op(nc.vector.memset, None, packs[:, :, :], 0.0)
            for i, pack in enumerate((PACK1, PACK2)):
                r = 0
                for name, n in pack:
                    if name in ("diff_q_norm", "k_norm"):
                        for h in range(2):
                            m_pack = load(packs[r:r + 1, i, h * HEAD:(h + 1) * HEAD], K["flat_" + name],
                                          c_pack, clear)
                    else:
                        m_pack = load(packs[r:r + n, i, :], K["flat_" + name], c_pack, clear)
                    r += n
            b = take_bank()
            for i in range(2):
                m = turn(ps[:, b, i * P:(i + 1) * P], packs[:, i], [m_pack, consts])
            m_vec = copy(vecs[:, :], ps[:, b, 0:2 * P], m)
            bank_free[b] = m_vec
            for q in (act, dve, pool, pe):
                q.wait(m_vec, consts)
            for k in range(KC):
                b = take_bank()
                for tb in range(TB):
                    m = turn(ps[:, b, tb * P:(tb + 1) * P], x_in[:, tb, k * P:(k + 1) * P],
                             [m_x, consts, bank_free[b]])
                x_marks[k] = bank_free[b] = copy(x[:, k], ps[:, b], m)
                feed(k, "ffn_norm")
        fence()

        def ffn_buffers(tag, on):
            return Operand(f"hidden_{tag}", KF // 2 + 1, on), sb(f"ffn_tmp_{tag}", [P, 3, 3, T], on=on), [None] * 3

        def ffn(parts, buffers, final, new_rms=True):
            hidden, tmp, tmp_used = buffers
            gate_mark = [None] * 3

            def gate_up(bi, i, b, mark):
                s = (2 * bi + i % 2) % 3
                m = times_rstd(tmp[:, s, i // 2], b, mark, tmp_used[s])
                if i < 2:
                    gate_mark[s] = activation(tmp[:, s, 0], tmp[:, s, 0], ACT.Silu, m)
                    return m
                f = 2 * bi + i - 2
                g = tt(tmp[:, s, 2], tmp[:, s, 0], tmp[:, s, 1], ALU.mult, [gate_mark[s], m])
                tmp_used[s] = hidden.put(f, tmp[:, s, 2], g)
                return m

            def add(bi, i, b, mark):
                k = 4 * bi + i
                m = x_marks[k] = stt(x[:, k], ps[:, b], 0.5, x[:, k], ALU.mult, ALU.add,
                                     [mark, x_marks[k], x_read[k]])
                if down is parts[-1][1]:
                    final(k)
                return m

            if new_rms:
                after_units(2, finish_x)
            for up, down in parts:
                linear(up, OP, gate_up)
                linear(down, hidden, add)

        with ExitStack() as ph:
            ffn(layer["ffn00"], ffn_buffers("ffn00", ph), feed)
        fence()

        MIX_R, MIX_K, MIX_V, MIX_W, MIX_A, MIX_G = range(6)
        with ExitStack() as ph:
            rkv = [sb(n, [P, KC, T], on=ph) for n in ("r", "k", "v")]
            lora = [sb(n, [P, T], on=ph) for n in ("lora_w_a", "lora_g", "lora_g_rest")]
            finish_x()
            with ExitStack() as ph2:
                h = sb("h_shifted", [P, KC, T + 1], on=ph2)
                dx = sb("dx", [P, KC, T], on=ph2)
                mixed = sb("mixed", [P, 4, T], on=ph2)
                first = dve.op(nc.vector.memset, None, h[:, :, 0:1], 0.0)
                dx_marks, h_marks = [], []
                for k in range(KC):
                    m = stt(h[:, k, 1:T + 1], x[:, k], vec("mix_norm", k), rstd[:, :], ALU.mult, ALU.mult,
                            [state["rstd"], x_marks[k]])
                    h_marks.append(m)
                    dx_marks.append(tt(dx[:, k], h[:, k, 0:T], h[:, k, 1:T + 1], ALU.subtract, [m, first]))
                mixed_used = [None] * 4

                def mix(k, which, slot):
                    return stt(mixed[:, slot], dx[:, k], vec("rwkv_mu", which * KC + k), h[:, k, 1:T + 1],
                               ALU.mult, ALU.add, [dx_marks[k], mixed_used[slot]])

                for n, which, outs in (("w1", MIX_W, ((0, 64, 0, lora[0], ACT.Tanh),)),
                                       ("a1", MIX_A, ((0, 64, 64, lora[0], ACT.Copy),)),
                                       ("g1", MIX_G, ((0, 128, 0, lora[1], ACT.Sigmoid), (128, 160, 0, lora[2], ACT.Sigmoid)))):
                    banks = [take_bank() for _ in outs]
                    for uid in layer[n][0]:
                        u = W.fetch(uid)
                        for kk in range(u["nk"]):
                            k = u["k0"] + kk
                            m = mix(k, which, k % 4)
                            for b, (c0, c1, p0, _, _) in zip(banks, outs):
                                mark = mm(ps[p0:p0 + c1 - c0, b], u["raw"][:, kk, c0:c1], mixed[:, k % 4],
                                          [m, u["ready"], bank_free[b] if k == 0 else None],
                                          start=k == 0, stop=k == KC - 1)
                            mixed_used[k % 4] = mark
                        W.done(u, mark)
                    for b, (c0, c1, p0, dst, func) in zip(banks, outs):
                        rows = slice(p0, p0 + c1 - c0)
                        bank_free[b] = activation(dst[rows, :], ps[rows, b], func, mark)
                lora_mark = act.now()
                def put_mixed(s):
                    def put(k):
                        mixed_used[k % 4] = OP.put(k, mixed[:, k % 4], mix(k, s, k % 4))
                    return put

                for k in range(KC):
                    put_mixed(0)(k)
                for s in range(3):
                    def keep(bi, i, b, mark, s=s):
                        return copy(rkv[s][:, 4 * bi + i], ps[:, b], mark, q=act)
                    linear(layer["rkv", s], OP, keep, freed=put_mixed(s + 1) if s < 2 else None)
            fence()

            HT = T // 2
            x_kept = nc.dram_tensor("x_kept", (P, KC, T), F32, kind="Internal").ap()
            kept = load(x_kept, x[:, :, :], c_spill, h_marks, x_read)
            with ExitStack() as ph2:
                masks = sb("masks", [P, 2, P], on=ph2)
                seed = sb("seed_masks", [P, 2, P], on=ph2)
                level = sb("level_masks", [P, 5, P], on=ph2)
                run = sb("scan_reset", [P, HT], on=ph2)
                carry = sb("state_carried", [P, 2, P], on=ph2)
                rate = sb("rate", [P, 2, T], on=ph2)
                stat = sb("wkv_stat", [P, 2, 12], on=ph2)
                ar_ = sb("a_r_turned", [P, 2, 2, 2, P], on=ph2)
                bk_ = sb("b_k_turned", [P, 2, 2, HT], on=ph2)
                av_ = sb("a_nv", [P, 2, 4, P], on=ph2)
                nat_ = sb("b_k_v_natural", [P, 2, 3, 2, P], on=ph2)
                mq_ = sb("m_q", [P, 2, 4, 2, P], on=ph2)
                nq_ = sb("n_q", [P, 2, 4, 2, P], on=ph2)
                w_ = sb("w", [P, 2, 4, P], on=ph2)
                for dst, n in ((masks, "masks"), (seed, "seed"), (level, "level")):
                    load(dst[:, :, :], K[n].rearrange("p (a b) -> p a b", b=P), c_mask)
                m_masks = load(run[:, :], K["run"], c_mask)
                ident4, neg_ident = OP.lo[:, 2], OP.lo[:, 3, 0:P]
                m = pool.op(nc.gpsimd.memset, None, carry[:, :, :], 0.0)
                for j in range(4):
                    i_mark = copy(ident4[:, j * P:(j + 1) * P], ident[:, :], m)
                i_mark = ts(neg_ident, ident[:, :], -1.0, None, ALU.mult, None, i_mark)
                identr = ident4[:, 0:P]
                for q in (dve, pe, pool, act):
                    q.wait(m_masks, i_mark, kept)
                chunks = lambda a: a.rearrange("p (c t) -> p c t", t=CHUNK)
                blocks = lambda a: a.rearrange("p (b t) -> p b t", t=P)
                r_all, k_all, v_all = rkv
                y_marks = [None] * KC
                small_out = [None, None]

                def keep_bank(b, mark):
                    bank_free[b] = mark
                    return mark

                def narrow(name, m, rows_list):
                    b = take_bank()
                    ids = layer[name, m][0]
                    for j, (uid, rhs) in enumerate(zip(ids, rows_list)):
                        u = W.fetch(uid)
                        p0, n = u["base"], u["part"]
                        mark = mm(ps[:, b], u["raw"][p0:p0 + n, 0, 0:P], rhs[p0:p0 + n, :],
                                  [u["ready"], lora_mark, bank_free[b]], start=j == 0, stop=j == len(ids) - 1)
                        W.done(u, mark)
                    return b, mark

                def work(lane, m, half, before):
                    t = [x[:, 4 * lane + i // 2, (i % 2) * HT:(i % 2 + 1) * HT] for i in range(8)]
                    tokens = slice(half * HT, (half + 1) * HT)
                    r, k, v = r_all[:, m, tokens], k_all[:, m, tokens], v_all[:, m, tokens]
                    lwt, at, gt = (rstd, sq_sum)[lane][:, :], rate[:, lane], sq[:, lane]
                    ar, bt, kt = ar_[:, lane], bk_[:, lane, 0], bk_[:, lane, 1]
                    av, w, mq, nq = av_[:, lane], w_[:, lane], mq_[:, lane], nq_[:, lane]
                    bn, kn, vn = (nat_[:, lane, i] for i in range(3))
                    inv, inv_t, xm, mh = (blocks(OP.hi[:, 4 * lane + i]) for i in range(4))
                    ml = blocks(OP.lo[:, lane])
                    gbd, hbd, sbd, full = nq[:, :, 0, :], mq[:, :, 0, :], av, mq[:, :, 0, :]
                    sm = stat[:, lane]
                    f32 = lambda a: a.bitcast(F32)
                    if half == 0:
                        b, mk = narrow("w2", m, [lora[0]])
                        z = keep_bank(b, activation(lwt, ps[:, b], ACT.Sigmoid, [mk, before],
                                                    bias=vec("rwkv_w0", m)))
                        b, mk = narrow("a2", m, [lora[0]])
                        a = keep_bank(b, activation(at, ps[:, b], ACT.Sigmoid, [mk, before],
                                                    bias=vec("rwkv_a0", m)))
                        b, mk = narrow("g2", m, [lora[1], lora[2]])
                        g = keep_bank(b, copy(gt, ps[:, b], [mk, before], q=act))
                        lw = ts(lwt, lwt, -math.exp(-0.5), None, ALU.mult, None, z)
                        small_out[lane] = (lw, a, g)
                        yield
                    lw, a, g = small_out[lane]
                    lw_t, a_t = lwt[:, tokens], at[:, tokens]
                    cs = dve.op(nc.vector.tensor_tensor_scan, [lw, before], t[1], run[:, :], lw_t, 0.0,
                                ALU.mult, ALU.add)
                    cl = tt(t[6], t[1], lw_t, ALU.subtract, [cs, before])
                    s = activation(t[7], k, ACT.Square, before, scale=vec("rwkv_k_k", m))
                    b = take_bank()
                    mk = mm(ps[:, b, 0:HT], headsum[:, :], t[7], [s, bank_free[b]])
                    ep = activation(t[2], t[1], ACT.Exp, [cs, before])
                    en = activation(t[3], t[1], ACT.Exp, [cs, before], scale=-1.0)
                    ea = activation(t[6], t[6], ACT.Exp, cl)
                    n2 = keep_bank(b, ts(t[7], ps[:, b, 0:HT], 1e-24, None, ALU.max, None, mk))
                    yield
                    n2 = inv_sqrt(t[7], t[7], 1.0, EPS_NONE, n2)
                    yield
                    am = ts(t[4], a_t, -1.0, vec("rwkv_k_a", m), ALU.add, ALU.mult, [a, before])
                    k2 = stt(t[4], t[4], 1.0, k, ALU.add, ALU.mult, am)
                    kk = stt(t[5], k, vec("rwkv_k_k", m), t[7], ALU.mult, ALU.mult, n2)
                    m_a = stt(ar[:, :, 0, :], blocks(t[5]), -1.0, blocks(t[6]), ALU.mult, ALU.mult, [kk, ea])
                    yield
                    ka = tt(t[7], t[5], a_t, ALU.mult, kk)
                    m_b = tt(bt, t[7], t[3], ALU.mult, [ka, en])
                    m_k = tt(kt, t[4], t[3], ALU.mult, [k2, en])
                    m_r = tt(ar[:, :, 1, :], blocks(r), blocks(t[2]), ALU.mult, ep)
                    yield
                    last = chunks(t[2])[:, :, CHUNK - 1:CHUNK]
                    b2 = tt(chunks(t[0]), chunks(bt), last.broadcast_to([P, 4, CHUNK]), ALU.mult, [m_b, ep], q=pool)
                    k3 = tt(chunks(t[1]), chunks(kt), last.broadcast_to([P, 4, CHUNK]), ALU.mult, [m_k, ea, en],
                            q=pool)

                    def pairs(lhs, dst, mark):
                        marks_ = []
                        for e in range(2):
                            b = take_bank()
                            h0 = e * HEAD
                            for tb in range(2):
                                mk = mm(ps[:, b, tb * 256:(tb + 1) * 256], lhs[h0:h0 + HEAD, tb * P:(tb + 1) * P],
                                        ar[h0:h0 + HEAD, tb, :, :], [mark, m_a, m_r, bank_free[b]])
                            marks_.append(keep_bank(b, tt(
                                dst[:, 2 * e:2 * e + 2], ps[:, b].rearrange("p (q a t) -> p q a t", q=2, a=2),
                                masks[:, :, :].unsqueeze(1).broadcast_to([P, 2, 2, P]), ALU.mult, mk)))
                        return marks_
                    m_mq = pairs(bt, mq, m_b)
                    i4 = f32(ident4).rearrange("p (b t) -> p b t", t=P)
                    bx = [take_bank(), take_bank()]
                    for e in range(2):
                        h0 = e * HEAD
                        for tb in range(2):
                            mk = mm(ps[:, bx[e], tb * P:(tb + 1) * P], ar[h0:h0 + HEAD, tb, 0, :],
                                    bt[h0:h0 + HEAD, tb * P:(tb + 1) * P], [m_a, m_b, bank_free[bx[e]]])
                    for e in range(2):
                        o = keep_bank(bx[e], tt(inv[:, 2 * e:2 * e + 2], blocks(ps[:, bx[e], 0:HT]),
                                                seed[:, 0].unsqueeze(1).broadcast_to([P, 2, P]), ALU.mult, mk))
                    m_inv = tt(inv, f32(inv), i4, ALU.add, o, q=pool)
                    o = tt(inv_t, mq[:, :, 0, :], seed[:, 1].unsqueeze(1).broadcast_to([P, 4, P]), ALU.mult, m_mq,
                           q=pool)
                    m_invt = tt(inv_t, f32(inv_t), i4, ALU.add, o, q=pool)
                    h_ = activation(mh, mq[:, :, 0, :], ACT.Copy, m_mq)
                    l_ = tt(ml, mq[:, :, 0, :], f32(mh), ALU.subtract, h_)
                    m_m = [h_, l_]
                    yield
                    others = [("n", None), ("nat", 0), ("nat", 1), ("nat", 2), ("v", None)]
                    nat_marks = []
                    for lv in range(5):
                        b = take_bank()
                        for p in range(4):
                            mk = mm(ps[:, b, p * P:(p + 1) * P], mh[:, p], inv[:, p], [m_m[0], m_inv, bank_free[b]])
                        m_x = keep_bank(b, tt(xm, blocks(ps[:, b]), level[:, lv].unsqueeze(1).broadcast_to([P, 4, P]),
                                              ALU.mult, [mk, m_invt]))
                        if lv == 0:
                            m_nq = pairs(kt, nq, m_k)
                        else:
                            src, mark, i = ((ar[:, :, 0, :], m_a, 0), (blocks(t[0]), b2, 0), (blocks(t[1]), k3, 1),
                                            (blocks(v), None, 2))[lv - 1] if lv < 5 else None
                            b = take_bank()
                            for tb in range(2):
                                mk = turn(ps[:, b, tb * P:(tb + 1) * P], src[:, tb], [mark, bank_free[b]])
                            if lv == 1:
                                for e in range(2):
                                    o = copy(av[:, 2 * e:2 * e + 2, 0:HEAD],
                                             blocks(ps[:, b, 0:HT])[:, :, e * HEAD:(e + 1) * HEAD], mk, q=act)
                            else:
                                o = copy((bn, kn, vn)[i], blocks(ps[:, b, 0:HT]), mk, q=act)
                            nat_marks.append(keep_bank(b, o))
                        yield
                        bt_, bi_ = take_bank(), take_bank()
                        mm(ps[:, bt_], identr, f32r(inv_t), [m_invt, bank_free[bt_], i_mark], stop=False, mark=False,
                           skip_group_check=True)
                        for p in range(4):
                            mk = mm(ps[:, bt_, p * P:(p + 1) * P], xm[:, p], inv_t[:, p], m_x, start=False,
                                    skip_group_check=True)
                        mm(ps[:, bi_], identr, f32r(inv), [m_inv, bank_free[bi_]], stop=False, mark=False,
                           skip_group_check=True)
                        for p in range(4):
                            mk = mm(ps[:, bi_, p * P:(p + 1) * P], inv_t[:, p], xm[:, p], m_x, start=False,
                                    skip_group_check=True)
                        m_inv = keep_bank(bi_, activation(inv, blocks(ps[:, bi_]), ACT.Copy, mk))
                        m_invt = keep_bank(bt_, activation(inv_t, blocks(ps[:, bt_]), ACT.Copy, mk))
                        yield
                    b = take_bank()
                    mm(ps[:, b], identr, ident4, bank_free[b], stop=False, mark=False, skip_group_check=True)
                    mm(ps[:, b], neg_ident, f32r(inv), m_inv, start=False, stop=False, mark=False,
                       skip_group_check=True)
                    for p in range(4):
                        for part in (mh, ml):
                            mk = mm(ps[:, b, p * P:(p + 1) * P], part[:, p], inv[:, p], m_m, start=False,
                                    skip_group_check=True)
                    m_x = keep_bank(b, activation(xm, blocks(ps[:, b]), ACT.Copy, mk))
                    b = take_bank()
                    for p in range(4):
                        e, tb = p // 2, p % 2
                        mk = mm(ps[:, b, p * HEAD:(p + 1) * HEAD], nq[:, p, 0, :],
                                vn[:, tb, e * HEAD:(e + 1) * HEAD], [m_nq, nat_marks[3], bank_free[b]])
                    m_nv = keep_bank(b, copy(av[:, :, HEAD:P], ps[:, b, 0:HT].rearrange("p (q v) -> p q v", q=4), mk))
                    yield
                    b = take_bank()
                    mm(ps[:, b], identr, f32r(inv_t), [m_invt, bank_free[b]], stop=False, mark=False,
                       skip_group_check=True)
                    for p in range(4):
                        mk = mm(ps[:, b, p * P:(p + 1) * P], xm[:, p], inv_t[:, p], m_x, start=False,
                                skip_group_check=True)
                    m_full = keep_bank(b, copy(full, blocks(ps[:, b]), mk, q=act))
                    m_g = tt(gbd, ident[:, :].unsqueeze(1).broadcast_to([P, 4, P]), last.broadcast_to([P, 4, P]),
                             ALU.mult, m_nv, q=pool)
                    yield
                    b = take_bank()
                    for p in range(4):
                        mk = mm(ps[:, b, p * P:(p + 1) * P], full[:, p], av[:, p],
                                [m_full, m_nv, nat_marks[0], bank_free[b]])
                    m_w = keep_bank(b, copy(w, blocks(ps[:, b]), mk, q=act))
                    clear_h = pool.op(nc.gpsimd.memset, [m_w], hbd, 0.0)
                    bonus = stt(t[6], r, vec("rwkv_r_k", m), t[4], ALU.mult, ALU.mult, [k2, m_a])
                    yield
                    b = take_bank()
                    mk = mm(ps[:, b, 0:HT], headsum[:, :], t[6], [bonus, bank_free[b]])
                    m_bonus = keep_bank(b, tt(t[6], ps[:, b, 0:HT], v, ALU.mult, mk))
                    m_gh = []
                    for j in range(2):
                        b = take_bank()
                        j0 = j * HEAD
                        for tb in range(2):
                            for e in range(2):
                                h0, p = e * HEAD, 2 * e + tb
                                mm(ps[h0:h0 + HEAD, b, tb * HEAD:(tb + 1) * HEAD], w[j0:j0 + HEAD, p, 0:HEAD],
                                   bn[j0:j0 + HEAD, tb, h0:h0 + HEAD], [m_w, nat_marks[1], bank_free[b]], mark=False)
                        for tb in range(2):
                            for e in range(2):
                                h0, p = e * HEAD, 2 * e + tb
                                o = ps[h0:h0 + HEAD, b, P + tb * HEAD:P + (tb + 1) * HEAD]
                                mm(o, bn[j0:j0 + HEAD, tb, h0:h0 + HEAD], w[j0:j0 + HEAD, p, HEAD:P], None,
                                   stop=False, mark=False)
                                mk = mm(o, kn[j0:j0 + HEAD, tb, h0:h0 + HEAD], vn[j0:j0 + HEAD, tb, h0:h0 + HEAD],
                                        [nat_marks[2], nat_marks[3]], start=False)
                        for e in range(2):
                            h0 = e * HEAD
                            gv = gbd[h0:h0 + HEAD, j::2, h0:h0 + HEAD]
                            hv = hbd[h0:h0 + HEAD, j::2, h0:h0 + HEAD]
                            pv = ps[h0:h0 + HEAD, b, 0:2 * P].rearrange("p (g b n) -> p g b n", g=2, b=2)
                            m_gh.append(tt(gv, pv[:, 0], gv, ALU.add, [mk, m_g]))
                            m_gh.append(copy(hv, pv[:, 1], [mk, clear_h]))
                        keep_bank(b, m_gh[-1])
                    yield
                    b = take_bank()
                    for p in range(4):
                        e, tb = p // 2, p % 2
                        mk = mm(ps[e * HEAD:(e + 1) * HEAD, b, tb * P:(tb + 1) * P], w[:, p, 0:HEAD],
                                mq[:, p, 1, :], [m_w, bank_free[b]])
                    m_z = keep_bank(b, tt(blocks(t[3]), blocks(ps[:, b, 0:HT]), ar[:, :, 1, :], ALU.add, mk))
                    s_marks = [copy(sbd[:, 0], carry[:, lane], [m_w], q=pool) if half else None]
                    for c in range(4):
                        dst = sbd[:, c + 1] if c < 3 else carry[:, lane]
                        if c == 3 and half:
                            break
                        if c == 0 and not half:
                            s_marks.append(copy(dst, hbd[:, 0], [m_gh, clear_h]))
                            continue
                        yield
                        b = take_bank()
                        mk = mm(ps[:, b, 0:P], gbd[:, c], sbd[:, c], [s_marks[c], m_gh, clear_h, bank_free[b]])
                        s_marks.append(keep_bank(b, tt(dst, ps[:, b, 0:P], hbd[:, c], ALU.add, [mk, s_marks[0]])))
                    yield
                    b = take_bank()
                    opened = False
                    for tb in range(2):
                        for e in range(2):
                            p = 2 * e + tb
                            o = ps[:, b, tb * P + e * HEAD:tb * P + (e + 1) * HEAD]
                            mm(o, mq[:, p, 1, :], w[:, p, HEAD:P], bank_free[b], start=not opened, stop=False,
                               mark=False, skip_group_check=True)
                            opened = True
                            mk = mm(o, nq[:, p, 1, :], vn[:, tb, e * HEAD:(e + 1) * HEAD], None, start=False,
                                    stop=False, skip_group_check=True)
                    for c in range(4):
                        if c or half:
                            j0 = (c % 2) * CHUNK
                            mk = mm(ps[j0:j0 + CHUNK, b, (c // 2) * P:(c // 2 + 1) * P],
                                    t[3][:, c * CHUNK:(c + 1) * CHUNK], sbd[:, c], [s_marks[c], m_z], start=False,
                                    stop=c == 3, skip_group_check=True)
                    heads_ = lambda a_: a_.rearrange("p (q n) -> p q n", n=HEAD)
                    o = dve.op(nc.vector.tensor_reduce, mk, sm[:, 0:4], heads_(ps[:, b, 0:HT]), AX_X, ALU.add)
                    o = ts(sm[:, 4:8], sm[:, 0:4], -1.0 / HEAD, None, ALU.mult, None, o)
                    yc = keep_bank(b, tt(heads_(t[1]), heads_(ps[:, b, 0:HT]),
                                         sm[:, 4:8].unsqueeze(2).broadcast_to([P, 4, HEAD]), ALU.add, o))
                    s = activation(t[2], t[1], ACT.Square, [yc, m_gh])
                    yield
                    o = dve.op(nc.vector.tensor_reduce, s, sm[:, 0:4], heads_(t[2]), AX_X, ALU.add)
                    o = inv_sqrt(sm[:, 8:12], sm[:, 0:4], 1.0 / HEAD, EPS_RWKV, o)
                    yn = tt(heads_(t[1]), heads_(t[1]), sm[:, 8:12].unsqueeze(2).broadcast_to([P, 4, HEAD]),
                            ALU.mult, o)
                    yield
                    b = take_bank()
                    for tb in range(2):
                        mk = turn(ps[:, b, tb * P:(tb + 1) * P], t[1][:, tb * P:(tb + 1) * P], [yn, bank_free[b]])
                    y = keep_bank(b, activation(t[5], ps[:, b, 0:HT], ACT.Identity, mk, scale=vec("rwkv_ln_g", m),
                                                bias=vec("rwkv_ln_b", m)))
                    y = tt(t[5], t[5], t[6], ALU.add, [y, m_bonus])
                    y_marks[m] = tt(r, t[5], gt[:, tokens], ALU.mult, [y, g])
                    last_mark[lane] = y_marks[m]
                    yield

                f32r = lambda a: a.rearrange("p q t -> p (q t)")
                last_mark = [None, None]

                def lane_of(lane):
                    for m in range(lane, KC, 2):
                        for half in range(2):
                            yield from work(lane, m, half, last_mark[lane])

                lanes = [lane_of(0), lane_of(1)]
                for _ in range(WKV_SKEW):
                    next(lanes[0])
                live = list(lanes)
                while live:
                    for g_ in list(live):
                        if next(g_, "ended") == "ended":
                            live.remove(g_)
            fence()
            m_back = load(x[:, :, :], x_kept, c_spill)
            for k in range(KC):
                x_marks[k] = m_back
                x_read[k] = None
            for m in range(KC):
                OP.put(m, r_all[:, m], y_marks[m])

            def add_and_feed(blocks, gain, k0):
                def evac(bi, i, b, mark):
                    k = 4 * bi + i
                    m = x_marks[k] = tt(x[:, k], ps[:, b], x[:, k], ALU.add, [mark, x_marks[k], x_read[k]])
                    feed(k)
                    return m

                def refill(k):
                    for k in ([k] if k < 4 else range(4, KC) if k == KC - 1 else []):
                        x_read[k].append(OP.put(k, x[:, k], x_marks[k], vec(gain, k0 + k))[0])
                linear(blocks, OP, evac, freed=refill)
            add_and_feed(layer["rwkv_o"], "ffn_norm", KC)
        fence()

        with ExitStack() as ph:
            kT = sb("diff_keys", [P, KC, T], on=ph)
            V = sb("diff_values", [P, TB, C], on=ph)
            kv_tmp = sb("kv_tmp", [P, T], on=ph)
            rcol = sb("rstd_column", [P, TB], on=ph)
            with ExitStack() as ph2:
                buffers = ffn_buffers("ffn_mid", ph2)
                ffn(layer["ffn01"], buffers, lambda k: feed(k, "kv_norm"))

                def start_kv():
                    finish_x()
                    b = take_bank()
                    for tb in range(TB):
                        mk = mm(ps[:, b, tb:tb + 1], rstd[0:1, tb * P:(tb + 1) * P], ones[0:1, 0:1],
                                [state["rstd"], bank_free[b]])
                    state["rcol"] = bank_free[b] = copy(rcol[:, :], ps[:, b, 0:TB], mk)

                def keys(bi, i, b, mark):
                    k = 4 * bi + i
                    m = times_rstd(kT[:, k], b, mark)
                    after_units(1, lambda: head_norm(kT[:, k], vec("k_norm"), kv_tmp[:, :], m))
                    return m

                def values(bi, i, b, mark):
                    return ts(V[:, i, bi * T:(bi + 1) * T], ps[:, b], rcol[:, i:i + 1], None, ALU.mult, None,
                              [mark, state["rcol"]])

                def put_ffn(k):
                    x_read[k] = OP.put(k, x[:, k], x_marks[k], vec("ffn_norm", 2 * KC + k))[0]
                after_units(2, start_kv)
                linear(layer["kv"][0:2], OP, keys)
                linear(layer["kv"][2:4], OP, values, natural=True, freed=put_ffn)
                ffn(layer["ffn10"], buffers, lambda k: feed(k, "mix_norm", KC), new_rms=False)
            fence()

            LAM_INIT = 0.8 - 0.6 * math.exp(-0.3 * 1)
            with ExitStack() as ph2:
                q = sb("diff_queries", [P, KC, T], on=ph2)

                def queries(bi, i, b, mark):
                    k = 4 * bi + i
                    m = times_rstd(q[:, k], b, mark)
                    after_units(1, lambda: head_norm(q[:, k], vec("diff_q_norm"), kv_tmp[:, :], m))
                    return m
                after_units(2, finish_x)
                linear(layer["q"], OP, queries)
                flush_later()
                fence()
                dist = sb("distance", [P, T], on=ph2)
                lam = sb("lambda", [P, 4 * HEAD + 8], on=ph2)
                small_ = sb("diff_small", [P, 4, 12], on=ph2)
                subln = sb("subln", [P, 1], on=ph2)
                S = sb("diff_scores", [P, 4, 2, T], on=ph2)
                aT = sb("diff_probs_turned", [P, 4, T], on=ph2)
                O = sb("diff_out", [P, 4, TB, P], on=ph2)
                m_dist = load(dist[:, :], K["dist"], c_mask)
                m_lam = load(lam[0:1, 0:4 * HEAD], K["flat_diff_lambda"], c_lam)
                b = take_bank()
                mk = mm(ps[:, b, 0:256], ones[0:1, :], lam[0:1, 0:256], [m_lam, bank_free[b]])
                mk = bank_free[b] = copy(lam[:, 0:256], ps[:, b, 0:256], mk)
                for j in range(2):
                    o = lam[:, 128 * j:128 * j + 64]
                    mk = tt(o, o, lam[:, 128 * j + 64:128 * j + 128], ALU.mult, mk)
                    mk = dve.op(nc.vector.tensor_reduce, mk, lam[:, 256 + j:257 + j], o, AX_X, ALU.add)
                mk = activation(lam[:, 258:260], lam[:, 256:258], ACT.Exp, mk)
                mk = tt(lam[:, 260:261], lam[:, 259:260], lam[:, 258:259], ALU.subtract, mk)
                m_nlam = ts(lam[:, 261:262], lam[:, 260:261], -LAM_INIT, None, ALU.add, None, mk)
                m_subln = ts(subln[:, :], vec("diff_subln"), 1.0 - LAM_INIT, None, ALU.mult, None, None)

                def diff_head(h):
                    def steps(lane):
                        A, B = 2 * lane, 2 * lane + 1
                        s0 = 8.0 * 2.0 ** (-(h + 1))
                        sm = small_[:, lane]
                        o_marks = []
                        for tb in range(TB):
                            n = (tb + 1) * P
                            e_marks = []
                            for c, b in ((0, A), (1, B)):
                                r0 = c * HEAD
                                mk = mm(ps[:, b, 0:n], q[r0:r0 + HEAD, h, tb * P:(tb + 1) * P],
                                        kT[r0:r0 + HEAD, h, 0:n], [bank_free[b]])
                                bank_free[b] = stt(S[:, lane, c, 0:n], dist[:, (TB - 1 - tb) * P:T], s0,
                                                   ps[:, b, 0:n], ALU.mult, ALU.add, [mk, m_dist, lane_free[lane]])
                            yield
                            for c, b in ((0, A), (1, B)):
                                m = dve.op(nc.vector.tensor_reduce, bank_free[b], sm[:, c:c + 1],
                                           S[:, lane, c, 0:n], AX_X, ALU.max)
                                m = ts(sm[:, 2 + c:3 + c], sm[:, c:c + 1], -0.125, None, ALU.mult, None, m)
                                e_marks.append(activation(S[:, lane, c, 0:n], S[:, lane, c, 0:n], ACT.Exp, m,
                                                          bias=sm[:, 2 + c:3 + c], scale=0.125,
                                                          accum_out=sm[:, 4 + c:5 + c]))
                            yield
                            m = dve.op(nc.vector.reciprocal, e_marks, sm[:, 6:8], sm[:, 4:6])
                            m1 = tt(sm[:, 8:9], sm[:, 7:8], lam[:, 261:262], ALU.mult, [m, m_nlam])
                            m = ts(S[:, lane, 0, 0:n], S[:, lane, 0, 0:n], sm[:, 6:7], None, ALU.mult, None, m)
                            m = stt(S[:, lane, 0, 0:n], S[:, lane, 1, 0:n], sm[:, 8:9], S[:, lane, 0, 0:n],
                                    ALU.mult, ALU.add, [m, m1])
                            yield
                            for kt_ in range(tb + 1):
                                mk = turn(ps[:, A, kt_ * P:(kt_ + 1) * P], S[:, lane, 0, kt_ * P:(kt_ + 1) * P],
                                          [m, bank_free[A]])
                            lane_free[lane] = mk
                            m = bank_free[A] = copy(aT[:, lane, 0:n], ps[:, A, 0:n], mk, q=act)
                            yield
                            for kt_ in range(tb + 1):
                                mk = mm(ps[:, B, 0:P], aT[:, lane, kt_ * P:(kt_ + 1) * P],
                                        V[:, kt_, h * P:(h + 1) * P], [m, bank_free[B]],
                                        start=kt_ == 0, stop=kt_ == tb)
                            m = bank_free[B] = copy(O[:, lane, tb], ps[:, B, 0:P], [mk, o_free[lane]], q=act)
                            o_marks.append(m)
                            yield
                        for tb in range(TB):
                            m = activation(aT[:, lane, tb * P:(tb + 1) * P], O[:, lane, tb], ACT.Square, o_marks,
                                           accum_out=small_[:, lane, tb:tb + 1])
                        m = inv_sqrt(small_[:, lane, 4:8], small_[:, lane, 0:4], 1.0 / P, EPS_SUBLN, m)
                        yield
                        for tb in range(TB):
                            m2 = ts(O[:, lane, tb], O[:, lane, tb], small_[:, lane, 4 + tb:5 + tb], None,
                                    ALU.mult, None, m)
                        for tb in range(TB):
                            mk = turn(ps[:, A, tb * P:(tb + 1) * P], O[:, lane, tb], [m2, bank_free[A]])
                        o_free[lane] = mk
                        yield
                        bank_free[A] = OP.put(h, ps[:, A], [mk, m_subln], subln[:, :])
                    return steps
                lane_free, o_free = [None] * 4, [None] * 4
                interleave([diff_head(h) for h in range(DIFF_HEADS)], 4)
                add_and_feed(layer["diff_o"], "ffn_norm", 3 * KC)
        fence()

        with ExitStack() as ph:
            ffn(layer["ffn11"], ffn_buffers("ffn11", ph), feed)
        fence()

        with ExitStack() as ph:
            mod = sb("modulation", [P, 24, 2], on=ph)
            gain = sb("mod_gain", [P, KC, 2], on=ph)
            hc = Operand("hc", KC, ph, width=CTX)
            h = OP
            with ExitStack() as ph2:
                sc = sb("silu_c", [P, KC, 2], on=ph2)
                row = sb("mod_rows", [2, 3 * C], on=ph2)
                c_in = sb("ctx_in", [P, CTX // P, C], on=ph2)
                cT = sb("ctx_turned", [P, KC, CTX], on=ph2)
                crstd = sb("ctx_rstd", [P, CTX], on=ph2)
                tmp = sb("mod_tmp", [P, 2, T], on=ph2)
                m_ctx = load(c_in[:, :, :], I["ctx_2"][0].rearrange("(b p) c -> p b c", p=P), c_ctx)
                for j, n in enumerate(("c_2", "c_ctx_2")):
                    m_sc = activation(sc[:, :, j], vecs[:, column[n]:column[n] + KC], ACT.Silu, None)
                for bi, ids in enumerate(layer["mod"]):
                    b = take_bank()
                    for uid in ids:
                        u = W.fetch(uid)
                        for kk in range(u["nk"]):
                            k = u["k0"] + kk
                            mk = mm(ps[0:2, b], sc[:, k], u["raw"][:, kk, :],
                                    [m_sc, u["ready"], bank_free[b] if k == 0 else None],
                                    start=k == 0, stop=k == KC - 1)
                        W.done(u, mk)
                    m_row = bank_free[b] = copy(row[:, bi * T:(bi + 1) * T], ps[0:2, b], mk, q=act)
                b = take_bank()
                for i in range(24):
                    mk = turn(ps[:, b, 2 * i:2 * i + 2], row[0:2, i * P:(i + 1) * P], [m_row, bank_free[b]])
                nb = column["b_mod_2"]
                m_mod = bank_free[b] = tt(mod[:, :, :], ps[:, b, 0:48].rearrange("p (i j) -> p i j", j=2),
                                          vecs[:, nb:nb + 24].unsqueeze(2).broadcast_to([P, 24, 2]), ALU.add, mk)
                ng = column["norm_g_2"]
                m_gain = stt(gain[:, :, :], mod[:, KC:2 * KC, :], 1.0,
                             vecs[:, ng:ng + KC].unsqueeze(2).broadcast_to([P, KC, 2]), ALU.add, ALU.mult, m_mod)
                ct_marks = []
                for k in range(KC):
                    b = take_bank()
                    for tb in range(CTX // P):
                        mk = turn(ps[:, b, tb * P:(tb + 1) * P], c_in[:, tb, k * P:(k + 1) * P], [m_ctx, bank_free[b]])
                    bank_free[b] = copy(cT[:, k], ps[:, b, 0:CTX], mk)
                    ct_marks.append(bank_free[b])
                finish_x()
                m_crstd = rms([(cT[:, k], ct_marks[k]) for k in range(KC)], crstd[:, :])
                used = [None, None]
                for j, (src, marks, rs, m_rs, opnd) in enumerate((
                        (x, x_marks, rstd, state["rstd"], h), (cT, ct_marks, crstd, m_crstd, hc))):
                    w = src.shape[2]
                    for k in range(KC):
                        o = tmp[:, k % 2, 0:w]
                        m = tt(o, src[:, k], rs[:, 0:w], ALU.mult, [marks[k], m_rs, used[k % 2]])
                        m = ts(o, o, gain[:, k, j:j + 1], mod[:, k, j:j + 1], ALU.mult, ALU.add, [m, m_gain])
                        used[k % 2] = opnd.put(k, o, m)
            fence()

            o_mla = sb("mla_out", [P, TB, T], on=ph)
            attn_small = sb("attn_small", [P, 4, 4], on=ph)
            LANES = 3

            def attention(name, head_scores, value, o_all, scale, on):
                probs = sb(f"{name}_probs", [P, LANES, KEYS], on=on)
                turned = sb(f"{name}_probs_turned", [P, LANES, KEYS], on=on)
                probs_used = [None] * LANES

                def head(hd):
                    def steps(lane):
                        A, B = 2 * lane, 2 * lane + 1
                        flat = ps[:, A:B + 1].rearrange("p a b -> p (a b)")
                        sm, pr, tu = attn_small[:, lane], probs[:, lane], turned[:, lane]
                        for tb in range(TB):
                            m = head_scores(hd, tb, A, B, [bank_free[A], bank_free[B]], lane)
                            yield
                            m = dve.op(nc.vector.tensor_reduce, m, sm[:, 0:1], flat[:, 0:KEYS], AX_X, ALU.max)
                            m = ts(sm[:, 1:2], sm[:, 0:1], -scale, None, ALU.mult, None, m)
                            m = activation(pr, flat[:, 0:KEYS], ACT.Exp, [m, probs_used[lane]],
                                           bias=sm[:, 1:2], scale=scale, accum_out=sm[:, 2:3])
                            yield
                            m_rs = dve.op(nc.vector.reciprocal, m, sm[:, 3:4], sm[:, 2:3])
                            for kt_ in range(KEYS // P):
                                mk = turn(flat[:, kt_ * P:(kt_ + 1) * P], pr[:, kt_ * P:(kt_ + 1) * P], m)
                            probs_used[lane] = mk
                            yield
                            m = copy(tu, flat[:, 0:KEYS], mk, q=act if tb % 2 else dve)
                            yield
                            for kt_ in range(KEYS // P):
                                mk = mm(ps[:, A, 0:MLA_V], tu[:, kt_ * P:(kt_ + 1) * P], value(hd, kt_), m,
                                        start=kt_ == 0, stop=kt_ == KEYS // P - 1)
                            bank_free[A] = bank_free[B] = ts(o_all[:, tb, hd * MLA_V:(hd + 1) * MLA_V],
                                                             ps[:, A, 0:MLA_V], sm[:, 3:4], None, ALU.mult,
                                                             None, [mk, m_rs])
                            yield
                    return steps
                return head

            with ExitStack() as ph2:
                ka = sb("mla_keys", [QK, MLA_HEADS, KEYS], on=ph2)
                qa = sb("mla_queries", [QK, MLA_HEADS, T], on=ph2)
                va = sb("mla_values", [P, KEYS // P, MLA_HEADS * MLA_V], on=ph2)
                with ExitStack() as ph3:
                    cosm = sb("cosines", [QK, T], on=ph3)
                    sinm = sb("sines", [QK, T], on=ph3)
                    swap = sb("swap", [QK, QK], on=ph3)
                    ckv = Operand("ckv", 1, ph3)
                    cckv = Operand("cckv", 1, ph3, width=CTX)
                    small = sb("mla_tmp", [P, 2, T], on=ph3)
                    with ExitStack() as ph4:
                        for dst, n in ((cosm, "cos"), (sinm, "sin"), (swap, "swap")):
                            m_rope = load(dst[:, :], K[n], c_mask)
                        for q_ in (dve, pe):
                            q_.wait(m_rope)
                        fence_tmp = [None, None]
                        def latent(opnd, width, k_at, rotate):
                            def evac(bi, i, b, mark):
                                if i == 0:
                                    m = copy(small[:, 0, 0:width], ps[:, b, 0:width], [mark, fence_tmp[0]])
                                    r = rms([(small[:, 0, 0:width], m)], dst=small[:, 1, 0:width], channels=P)
                                    n = tt(small[:, 0, 0:width], small[:, 0, 0:width], small[:, 1, 0:width], ALU.mult, r)
                                    fence_tmp[0] = opnd.put(0, small[:, 0, 0:width], n, vec("g_ckv_2"))
                                    return m
                                rows = slice(NOPE, QK)
                                dst = ka[rows, 0, k_at:k_at + width]
                                m0 = m = copy(dst, ps[rows, b, 0:width], mark)
                                if rotate:
                                    b2 = take_bank()
                                    mk = mm(ps[0:QK, b2, 0:width], swap[rows, :], dst, [m, bank_free[b2]])
                                    s = small[rows, 1, 0:width]
                                    m2 = bank_free[b2] = tt(s, ps[rows, b2, 0:width], sinm[rows, 0:width], ALU.mult,
                                                            [mk, fence_tmp[0]])
                                    m = tt(dst, dst, cosm[rows, 0:width], ALU.mult, mk)
                                    fence_tmp[0] = m = tt(dst, dst, s, ALU.add, [m, m2])
                                for j in range(1, MLA_HEADS):
                                    copy(ka[rows, j, k_at:k_at + width], dst, m, q=pool)
                                return m0
                            return evac
                        linear(layer["ckv"], h, latent(ckv, T, 0, True), tiles=[(0, P), (NOPE, QK)],
                               extra=(hc, latent(cckv, CTX, T, False)))

                        def key_part(k_at, width):
                            def evac(bi, i, b, mark):
                                return copy(ka[0:NOPE, 4 * bi + i, k_at:k_at + width], ps[0:NOPE, b, 0:width],
                                            mark, q=act)
                            return evac
                        linear(layer["uk"], ckv, key_part(0, T), extra=(cckv, key_part(T, CTX)))

                        def value_part(t0):
                            def evac(bi, i, b, mark):
                                return copy(va[:, t0 + i], ps[:, b], mark, q=act)
                            return evac
                        linear(layer["uv"], ckv, value_part(0), natural=True, extra=(cckv, value_part(TB)))
                    with ExitStack() as ph4:
                        cq = Operand("cq", 2, ph4)
                        raw_q = o_mla[:, 0:2]
                        raw_marks = [None, None]

                        def cq_part(bi, i, b, mark):
                            raw_marks[i] = copy(raw_q[:, i], ps[:, b], mark, q=act)
                            return raw_marks[i]
                        linear(layer["cq"], h, cq_part)
                        r = rms([(raw_q[:, i], raw_marks[i]) for i in range(2)], dst=small[:, 1],
                                channels=2 * P, after=[dve.now(), pool.now()])
                        for i in range(2):
                            m = tt(raw_q[:, i], raw_q[:, i], small[:, 1], ALU.mult, r)
                            cq.put(i, raw_q[:, i], m, vec("g_cq_2", i))

                        def q_part(bi, i, b, mark):
                            hd = 4 * bi + i
                            m0 = m = copy(qa[:, hd], ps[0:QK, b], mark, q=act)
                            b2 = take_bank()
                            mk = mm(ps[0:QK, b2], swap[:, :], qa[:, hd], [m, bank_free[b2]])
                            s = small[0:QK, hd % 2]
                            m2 = bank_free[b2] = tt(s, ps[0:QK, b2], sinm[:, :], ALU.mult, [mk, m])
                            m = tt(qa[:, hd], qa[:, hd], cosm[:, :], ALU.mult, [mk])
                            tt(qa[:, hd], qa[:, hd], s, ALU.add, [m, m2])
                            return m0
                        linear(layer["uq"], cq, q_part, tiles=[(i * QK, QK) for i in range(4)])
                fence()

                def mla_scores(hd, tb, A, B, free, lane):
                    l = qa[:, hd, tb * P:(tb + 1) * P]
                    mm(ps[:, A], l, ka[:, hd, 0:T], free)
                    return mm(ps[:, B, 0:CTX], l, ka[:, hd, T:KEYS], None)
                head = attention("mla", mla_scores, lambda hd, kt_: va[:, kt_, hd * MLA_V:(hd + 1) * MLA_V],
                                 o_mla, QK ** -0.5, ph2)
                interleave([head(hd) for hd in range(MLA_HEADS)], LANES)
            fence()

            o_na = sb("na_out", [P, TB, T], on=ph)
            with ExitStack() as ph2:
                kb = sb("na_keys", [P, 4, KEYS], on=ph2)
                qb = sb("na_queries", [P, 4, T], on=ph2)
                vb = sb("na_values", [P, KEYS // P, T], on=ph2)
                bias = sb("window_bias", [P, LANES, NA_OFF, GRID_W], on=ph2)
                wmask = sb("window_mask", [P, GRID_W], on=ph2)
                m_wmask = load(wmask[:, :], K["window"], c_mask)

                def turned_keys(k_at, width):
                    return lambda bi, i, b, mark: copy(kb[:, i, k_at:k_at + width], ps[:, b, 0:width], mark, q=act)
                linear(layer["kb"], h, turned_keys(0, T), extra=(hc, turned_keys(T, CTX)))

                def natural_values(t0):
                    return lambda bi, i, b, mark: copy(vb[:, t0 + i], ps[:, b], mark, q=act)
                linear(layer["vb"], h, natural_values(0), natural=True, extra=(hc, natural_values(TB)))

                linear(layer["qb"], h, lambda bi, i, b, mark: activation(
                    qb[:, i], ps[:, b], ACT.Copy, mark, scale=0.125))
                ready = [act.now()]
                bias_marks, bias_used = [None] * NA_HEADS, [None] * NA_HEADS

                def load_bias(hd):
                    s = hd % LANES
                    for parity in range(2):
                        src = I["rpb_2"][hd, :, 1 - parity:1 - parity + NA_OFF, :]
                        m = load(bias[parity * GRID_W:(parity + 1) * GRID_W, s], src, c_bias[s],
                                 bias_used[hd - LANES] if hd >= LANES else None)
                    wm = wmask[:, :].unsqueeze(1).broadcast_to([P, NA_OFF, GRID_W])
                    bias_marks[hd] = tt(bias[:, s], bias[:, s], wm, ALU.add,
                                        [m, m_wmask], q=pool)

                def na_scores(hd, tb, A, B, free, lane):
                    if tb == 0 and bias_marks[hd] is None:
                        load_bias(hd)
                    h0, kt_ = (hd % 2) * HEAD, hd // 2
                    l = qb[h0:h0 + HEAD, kt_, tb * P:(tb + 1) * P]
                    mk = mm(ps[:, A], l, kb[h0:h0 + HEAD, kt_, 0:T], [free, ready])
                    mk2 = mm(ps[:, B, 0:CTX], l, kb[h0:h0 + HEAD, kt_, T:KEYS], None)
                    e0 = NA_KR - 2 - 2 * tb
                    v = bias[:, hd % LANES, e0:e0 + NA_KR, :].rearrange("p e c -> p (e c)")
                    m = tt(ps[:, A], ps[:, A], v, ALU.add, [mk2, bias_marks[hd]])
                    bias_used[hd] = m
                    return m
                head = attention("na", na_scores, lambda hd, kt_: vb[:, kt_, hd * MLA_V:(hd + 1) * MLA_V],
                                 o_na, 1.0, ph2)
                interleave([head(hd) for hd in range(NA_HEADS)], LANES)
            fence()

            with ExitStack() as ph2:
                z = sb("silu_z", [P, 4, T], on=ph2)
                g = sb("sigmoid_g", [P, KC, T], on=ph2)
                y = sb("y", [P, KC, T], on=ph2)
                gated = Operand("gated", 4, ph2)
                gtmp = sb("gated_tmp", [P, 2, T], on=ph2)
                g_marks, y_marks = [None] * KC, [None] * KC
                g_used, z_used, gt_used = [None] * KC, [None] * 4, [None, None]
                for branch, (zn, gn, wn, o_all) in enumerate((("za", "ga", "w_oa", o_mla), ("zb", "gb", "w_ob", o_na))):
                    def silu_z(bi, i, b, mark):
                        z_marks[i] = activation(z[:, i], ps[:, b], ACT.Silu, [mark, z_used[i]])
                        return z_marks[i]

                    def sigmoid_g(bi, i, b, mark):
                        k = 4 * bi + i
                        g_marks[k] = activation(g[:, k], ps[:, b], ACT.Sigmoid, [mark, g_used[k]])
                        return g_marks[k]

                    def gate_y(bi, i, b, mark, branch=branch):
                        k = 4 * bi + i
                        if branch == 0:
                            g_used[k] = y_marks[k] = tt(y[:, k], ps[:, b], g[:, k], ALU.mult, [mark, g_marks[k]])
                            return y_marks[k]
                        m = tt(g[:, k], ps[:, b], g[:, k], ALU.mult, [mark, g_marks[k]])
                        y_marks[k] = tt(y[:, k], y[:, k], g[:, k], ALU.add, [m, y_marks[k]])
                        return m
                    z_marks = [None] * 4
                    linear(layer[zn], h, silu_z)
                    for k in range(4):
                        b = take_bank()
                        for tb in range(TB):
                            mk = turn(ps[:, b, tb * P:(tb + 1) * P], o_all[:, tb, k * P:(k + 1) * P], bank_free[b])
                        m = bank_free[b] = tt(gtmp[:, k % 2], ps[:, b], z[:, k], ALU.mult,
                                              [mk, z_marks[k], gt_used[k % 2]])
                        z_used[k] = m
                        gt_used[k % 2] = gated.put(k, gtmp[:, k % 2], m)
                    linear(layer[gn], h, sigmoid_g)
                    linear(layer[wn], gated, gate_y)
                for k in range(KC):
                    h.put(k, y[:, k], y_marks[k])

                def add_gated(bi, i, b, mark):
                    k = 4 * bi + i
                    x_marks[k] = stt(x[:, k], ps[:, b], mod[:, 2 * KC + k, 0:1], x[:, k], ALU.mult, ALU.add,
                                     [mark, x_marks[k], x_read[k]])
                    m = x_marks[k]
                    feed(k)
                    return m
                linear(layer["w_out"], h, add_gated)
        fence()

        with ExitStack() as ph:
            y = sb("normed", [P, KC, T], on=ph)
            o = sb("out_rows", [P, TB, C], on=ph)
            finish_x()
            for k in range(KC):
                m = stt(y[:, k], x[:, k], vec("final_g_2", k), rstd[:, :], ALU.mult, ALU.mult, state["rstd"])
                b = take_bank()
                for tb in range(TB):
                    mk = turn(ps[:, b, tb * P:(tb + 1) * P], y[:, k, tb * P:(tb + 1) * P], [m, bank_free[b]])
                m = bank_free[b] = copy(o[:, :, k * P:(k + 1) * P], ps[:, b].rearrange("p (b c) -> p b c", c=P), mk,
                                        q=act if k % 2 else dve)
            m_out = load(out[0].rearrange("(b p) c -> p b c", p=P), o[:, :, :], c_out, act.now(), dve.now())
            sp.wait(m_out)

        with nc.Block() as block:
            @block.sync
            def _(engine):
                sp.emit(engine)

            @block.scalar
            def _(engine):
                act.emit(engine)

            @block.vector
            def _(engine):
                dve.emit(engine)

            @block.gpsimd
            def _(engine):
                pool.emit(engine)

            @block.tensor
            def _(engine):
                pe.emit(engine)


def tables():
    i, j = np.arange(P)[:, None], np.arange(P)[None, :]
    same = i // CHUNK == j // CHUNK
    f = lambda a: np.ascontiguousarray(a, dtype=np.float32)
    heads = f(i // HEAD == j // HEAD)
    t = {"ident": f(i == j), "headsum": heads}
    t["masks"] = f(np.concatenate([same & (i < j), same & (i <= j)], 1))
    near = (i // 2 == j // 2)
    t["seed"] = f(np.concatenate([near & (i > j), near & (i < j)], 1))
    t["level"] = f(np.concatenate([(i // (2 * s) == j // (2 * s)) & (i % (2 * s) >= s) & (j % (2 * s) < s)
                                   for s in (2, 4, 8, 16, 32)], 1))
    t["run"] = f(np.broadcast_to(np.arange(T // 2) % CHUNK != 0, (P, T // 2)))
    d = np.arange(T)[None, :] - (T - P) - i
    t["dist"] = f(np.where(d > 0, NEG, d))
    half = ROPE // 4
    freqs = np.float32(10000.0) ** (-np.arange(half, dtype=np.float32) / np.float32(half))
    cos, sin = np.ones((QK, T), np.float32), np.zeros((QK, T), np.float32)
    swap = np.zeros((QK, QK), np.float32)
    tok = np.arange(T)
    for part, pos in enumerate((tok // GRID_W, tok % GRID_W)):
        ang = pos.astype(np.float32)[None, :] * freqs[:, None].astype(np.float32)
        base = NOPE + part * 2 * half
        for s in range(2):
            rows = slice(base + s * half, base + (s + 1) * half)
            cos[rows], sin[rows] = np.cos(ang), np.sin(ang)
        for c in range(half):
            swap[base + half + c, base + c] = -1.0
            swap[base + c, base + half + c] = 1.0
    t.update(cos=cos, sin=sin, swap=swap)
    col, start = np.arange(GRID_W), np.clip(np.arange(GRID_W) - NA_KC // 2, 0, GRID_W - NA_KC)
    inside = (col[None, :] >= start[:, None]) & (col[None, :] < start[:, None] + NA_KC)
    t["window"] = f(np.tile(np.where(inside, 0.0, NEG), (2, 1)))
    return t


_INS = ['x', 'ffn_norm', 'ffn_w_in', 'ffn_w_out', 'mix_norm', 'rwkv_mu', 'rwkv_w_rkv', 'rwkv_w0', 'rwkv_w1',
        'rwkv_w2', 'rwkv_a0', 'rwkv_a1', 'rwkv_a2', 'rwkv_g1', 'rwkv_g2', 'rwkv_k_k', 'rwkv_k_a', 'rwkv_r_k',
        'rwkv_ln_g', 'rwkv_ln_b', 'rwkv_w_o', 'kv_norm', 'w_kv', 'k_norm', 'diff_w_q', 'diff_q_norm',
        'diff_lambda', 'diff_subln', 'diff_w_o', 'c_2', 'ctx_2', 'c_ctx_2', 'w_mod_2', 'b_mod_2', 'norm_g_2',
        'w_in_2', 'g_cq_2', 'w_uq_2', 'g_ckv_2', 'w_ukv_2', 'rpb_2', 'w_oa_2', 'w_ob_2', 'w_out_2', 'final_g_2']
PAD = GRID_W - NA_KC


def kernel(**inputs):
    import concourse.bacc as _bacc
    from concourse.bass_utils import run_bass_kernel_spmd as _run

    nc = _bacc.Bacc("TRN2", target_bir_lowering=False, num_devices=1)
    arrays, aps = {}, {}

    def give(name, a):
        arrays[f"in_{name}_dram"] = np.ascontiguousarray(a)
        return nc.dram_tensor(f"in_{name}_dram", a.shape, mybir.dt.from_np(a.dtype), kind="ExternalInput").ap()

    for name in _INS:
        a = np.asarray(inputs[name])
        if name == "rpb_2":
            a = np.pad(a[0], ((0, 0), (0, 0), (PAD, PAD)))
            a = np.stack([a[:, :, GRID_W - 1 - w:2 * GRID_W - 1 - w] for w in range(GRID_W)], axis=1)
        aps[name] = give(name, a)
    consts = {n: give("table_" + n, a) for n, a in tables().items()}
    for name, n in PACK1 + PACK2 + [("diff_lambda", 1)]:
        ap = aps[name]
        while len(ap.shape) > 1:
            ap = ap.rearrange("a b -> (a b)" if len(ap.shape) == 2 else
                              "a b c -> (a b) c" if len(ap.shape) == 3 else "a b c d -> (a b) c d")
        size = ap.shape[0]
        rows = 1 if size < P or name == "diff_lambda" else n
        consts["flat_" + name] = ap.rearrange("(r c) -> r c", r=rows)
    out = nc.dram_tensor("out_0_dram", (1, T, C), F32, kind="ExternalOutput").ap()
    program(nc, aps, consts, out)
    r = _run(nc, [arrays], core_ids=[0])
    return r.results[0]["out_0_dram"]
```
